# Optimizing a Trainium2 kernel written in Bass

```python
import jax, jax.numpy as jnp
from jax import lax
import numpy as np
import math

D_MODEL = 2048
BATCH = 1
SEQ = 256
DEPTH = 1

PLE_DIM = 256
R_HEADS = 16
R_HEAD = 64
R_WIDTH = R_HEADS * R_HEAD
DECAY_LORA = 64
AAA_LORA = 64
GATE_LORA = 160
R_GN_EPS = 64e-5
RWKV_COLS = 3 * R_WIDTH + DECAY_LORA + AAA_LORA + GATE_LORA
M_HEADS = 8
M_QK = 64
M_V = 128
M_WIDTH = M_HEADS * M_V
CONV_K = 4
CHUNK = 128
M_NORM_EPS = 1e-6
MLSTM_COLS = 2 * M_HEADS * M_QK + 2 * M_WIDTH + 2 * M_HEADS
GATE_COLS = 2 * D_MODEL
IN_COLS = RWKV_COLS + MLSTM_COLS + GATE_COLS
N_GROUPS = 4
EXPERTS_PER_GROUP = 8
N_EXPERTS = N_GROUPS * EXPERTS_PER_GROUP
TOP_K = 2
D_EXPERT = 512
MOE_BLOCK = 128
LN_EPS = 1e-5
ALPHA = (2 * DEPTH) ** 0.25
BETA = (8 * DEPTH) ** -0.25


F32 = jnp.float32

def _split(t, sizes):
    return jnp.split(t, np.cumsum(sizes)[:-1].tolist(), axis=-1)

def _layer_norm(x, w, b):
    xf = x.astype(F32)
    mu = xf.mean(-1, keepdims=True)
    var = jnp.square(xf - mu).mean(-1, keepdims=True)
    return ((xf - mu) * lax.rsqrt(var + LN_EPS) * w + b).astype(x.dtype)

def _head_norm(y, eps):
    mu = y.mean(-1, keepdims=True)
    var = jnp.square(y - mu).mean(-1, keepdims=True)
    return (y - mu) * lax.rsqrt(var + eps)

def _causal_conv(t, w, b):
    seq = t.shape[1]
    tp = jnp.pad(t, ((0, 0), (CONV_K - 1, 0), (0, 0)))
    return b + sum(w[j] * tp[:, j:j + seq] for j in range(CONV_K))

def _rwkv7_scan(r, decay, k, v, kk, a):
    bsz, _, h, n = r.shape

    def step(state, inp):
        r_t, w_t, k_t, v_t, kk_t, a_t = inp
        s_kk = jnp.einsum('bhvk,bhk->bhv', state, kk_t)
        state = (state * w_t[:, :, None, :]
                 - s_kk[..., None] * (kk_t * a_t)[:, :, None, :]
                 + v_t[..., None] * k_t[:, :, None, :])
        return state, jnp.einsum('bhvk,bhk->bhv', state, r_t)

    xs = tuple(jnp.moveaxis(t, 1, 0) for t in (r, decay, k, v, kk, a))
    _, ys = lax.scan(step, jnp.zeros((bsz, h, n, n), F32), xs)
    return jnp.moveaxis(ys, 0, 1)

def _rwkv7_mixer(z, mu, w0, w_w2, a0, w_a2, w_g2, k_k, k_a, r_k, lnx_w, lnx_b):
    bsz, seq, _ = z.shape
    z_prev = jnp.pad(z, ((0, 0), (1, 0), (0, 0)))[:, :-1]
    z = z + mu * (z_prev - z)
    r, k, v, zw, za, zg = _split(z, [R_WIDTH, R_WIDTH, R_WIDTH, DECAY_LORA, AAA_LORA, GATE_LORA])
    w = -jax.nn.softplus(-(w0 + jnp.tanh(zw) @ w_w2).astype(F32)) - 0.5
    decay = jnp.exp(-jnp.exp(w))
    a = jax.nn.sigmoid((a0 + za @ w_a2).astype(F32))
    g = jax.nn.sigmoid(zg) @ w_g2
    heads = lambda t: t.astype(F32).reshape(bsz, seq, R_HEADS, R_HEAD)
    r, k, v, decay, a = heads(r), heads(k), heads(v), heads(decay), heads(a)
    kk = k * k_k.astype(F32).reshape(R_HEADS, R_HEAD)
    kk = kk / jnp.maximum(jnp.sqrt(jnp.sum(kk * kk, -1, keepdims=True)), 1e-12)
    k = k * (1.0 + (a - 1.0) * k_a.astype(F32).reshape(R_HEADS, R_HEAD))
    y = _rwkv7_scan(r, decay, k, v, kk, a)
    y = _head_norm(y, R_GN_EPS).reshape(bsz, seq, R_WIDTH) * lnx_w + lnx_b
    bonus = (jnp.sum(r * k * r_k.astype(F32), -1, keepdims=True) * v).reshape(bsz, seq, R_WIDTH)
    return ((y + bonus) * g).astype(z.dtype)

def _mlstm_chunkwise(q, k, v, i_pre, log_f):
    bsz, h, seq, dqk = q.shape
    dv = v.shape[-1]
    nc = seq // CHUNK

    def chunks(t):
        return jnp.moveaxis(t.reshape(t.shape[:2] + (nc, CHUNK) + t.shape[3:]), 2, 0)

    causal = jnp.tril(jnp.ones((CHUNK, CHUNK), bool))

    def step(carry, inp):
        c_st, n_st, m_st = carry
        q_c, k_c, v_c, i_c, f_c = inp
        a = jnp.cumsum(f_c, -1)
        a_tot = a[..., -1]
        d = jnp.where(causal, a[..., :, None] - a[..., None, :] + i_c[..., None, :], -jnp.inf)
        inter = a + m_st[..., None]
        m_t = jnp.maximum(inter, d.max(-1))
        s = jnp.einsum('bhtd,bhsd->bhts', q_c, k_c) * jnp.exp(d - m_t[..., None])
        ie = jnp.exp(inter - m_t)
        num = (ie[..., None] * jnp.einsum('bhtd,bhde->bhte', q_c, c_st)
               + jnp.einsum('bhts,bhse->bhte', s, v_c))
        den = ie * jnp.einsum('bhtd,bhd->bht', q_c, n_st) + s.sum(-1)
        h_c = num / jnp.maximum(jnp.abs(den), jnp.exp(-m_t))[..., None]
        gl = a_tot[..., None] - a + i_c
        m_new = jnp.maximum(a_tot + m_st, gl.max(-1))
        sc = jnp.exp(a_tot + m_st - m_new)
        ge = jnp.exp(gl - m_new[..., None])
        c_st = sc[..., None, None] * c_st + jnp.einsum('bhs,bhsd,bhse->bhde', ge, k_c, v_c)
        n_st = sc[..., None] * n_st + jnp.einsum('bhs,bhsd->bhd', ge, k_c)
        return (c_st, n_st, m_new), h_c

    init = (jnp.zeros((bsz, h, dqk, dv), F32), jnp.zeros((bsz, h, dqk), F32),
            jnp.full((bsz, h), -jnp.inf, F32))
    _, hs = lax.scan(step, init, tuple(chunks(t) for t in (q, k, v, i_pre, log_f)))
    return jnp.moveaxis(hs, 0, 2).reshape(bsz, h, seq, dv)

def _mlstm_mixer(z, conv_w, conv_b, i_bias, f_bias, mh_w):
    bsz, seq, _ = z.shape
    qk, v, ig, fg, o = _split(z, [2 * M_HEADS * M_QK, M_WIDTH, M_HEADS, M_HEADS, M_WIDTH])
    qk = jax.nn.silu(_causal_conv(qk, conv_w, conv_b))
    q, k = _split(qk, [M_HEADS * M_QK, M_HEADS * M_QK])
    heads = lambda t, d: t.astype(F32).reshape(bsz, seq, M_HEADS, d).transpose(0, 2, 1, 3)
    q, k, v = heads(q, M_QK), heads(k, M_QK) * M_QK ** -0.5, heads(v, M_V)
    i_pre = (ig + i_bias).astype(F32).transpose(0, 2, 1)
    log_f = jax.nn.log_sigmoid((fg + f_bias).astype(F32)).transpose(0, 2, 1)
    h = _mlstm_chunkwise(q, k, v, i_pre, log_f)
    h = _head_norm(h, M_NORM_EPS).transpose(0, 2, 1, 3).reshape(bsz, seq, M_WIDTH) * mh_w
    return (jax.nn.sigmoid(o) * h).astype(z.dtype)

def _hier_moe(xf, w_rg, b_rg, w_re, b_re, w_gate, w_up, w_down):
    n, d = xf.shape
    lg = (xf @ w_rg).astype(F32) + b_rg
    g_sel = jnp.argmax(lg, -1)
    g_w = jnp.take_along_axis(jax.nn.softmax(lg, -1), g_sel[:, None], -1)
    le = ((xf @ w_re).astype(F32) + b_re).reshape(n, N_GROUPS, EXPERTS_PER_GROUP)
    le = jnp.take_along_axis(le, g_sel[:, None, None], 1)[:, 0]
    top_l, top_i = lax.top_k(le, TOP_K)
    wts = jax.nn.softmax(top_l, -1) * g_w
    eid = (g_sel[:, None] * EXPERTS_PER_GROUP + top_i).reshape(-1)
    tok = jnp.repeat(jnp.arange(n, dtype=jnp.int32), TOP_K)
    wt = wts.reshape(-1)
    order = jnp.argsort(eid)
    eid_s, tok_s, wt_s = eid[order], tok[order], wt[order]
    counts = jnp.bincount(eid, length=N_EXPERTS)
    start = jnp.cumsum(counts) - counts
    padded = ((counts + MOE_BLOCK - 1) // MOE_BLOCK) * MOE_BLOCK
    pend = jnp.cumsum(padded)
    pstart = pend - padded
    n_rows = TOP_K * n
    dest = pstart[eid_s] + (jnp.arange(n_rows) - start[eid_s])
    nb = -(-n_rows // MOE_BLOCK) + N_EXPERTS
    rows = nb * MOE_BLOCK
    tok_rows = jnp.zeros((rows,), jnp.int32).at[dest].set(tok_s)
    wt_rows = jnp.zeros((rows,), F32).at[dest].set(wt_s)
    blk_e = jnp.minimum(jnp.searchsorted(pend, jnp.arange(nb) * MOE_BLOCK, side='right'),
                        N_EXPERTS - 1)

    def one_block(args):
        t_idx, e = args
        xb = xf[t_idx]
        hb = jax.nn.silu(xb @ w_gate[e]) * (xb @ w_up[e])
        return hb @ w_down[e]

    out = lax.map(one_block, (tok_rows.reshape(nb, MOE_BLOCK), blk_e)).reshape(rows, d)
    out = out * wt_rows[:, None].astype(out.dtype)
    return jnp.zeros_like(xf).at[tok_rows].add(out)

def first_inputs(seed: int = 0) -> dict:
    key = jax.random.key(seed)
    ks = iter(jax.random.split(key, 40))
    nrm = lambda shape, s: s * jax.random.normal(next(ks), shape, F32)
    uni = lambda shape, lo, hi: jax.random.uniform(next(ks), shape, F32, lo, hi)
    L, D = DEPTH, D_MODEL
    col_scale = jnp.concatenate([
        jnp.ones((2 * R_WIDTH,), F32), jnp.full((R_WIDTH,), BETA, F32),
        jnp.ones((RWKV_COLS - 3 * R_WIDTH + 2 * M_HEADS * M_QK,), F32),
        jnp.full((M_WIDTH,), BETA, F32),
        jnp.ones((2 * M_HEADS + M_WIDTH + GATE_COLS,), F32)])
    return {
        'x': nrm((BATCH, SEQ, D), 1.0),
        'p': nrm((L, BATCH, SEQ, PLE_DIM), 1.0),
        'w_in': nrm((L, D, IN_COLS), D ** -0.5) * col_scale,
        'mu_shift': uni((L, RWKV_COLS), 0.0, 1.0),
        'w0': uni((L, R_WIDTH), -6.0, -1.0),
        'w_w2': nrm((L, DECAY_LORA, R_WIDTH), 0.5 * DECAY_LORA ** -0.5),
        'a0': nrm((L, R_WIDTH), 0.1),
        'w_a2': nrm((L, AAA_LORA, R_WIDTH), 0.5 * AAA_LORA ** -0.5),
        'w_g2': nrm((L, GATE_LORA, R_WIDTH), GATE_LORA ** -0.5),
        'k_k': 0.85 + nrm((L, R_WIDTH), 0.05),
        'k_a': 1.0 + nrm((L, R_WIDTH), 0.05),
        'r_k': nrm((L, R_HEADS, R_HEAD), 0.1),
        'lnx_w': 1.0 + nrm((L, R_WIDTH), 0.05),
        'lnx_b': nrm((L, R_WIDTH), 0.01),
        'conv_w': nrm((L, CONV_K, 2 * M_HEADS * M_QK), CONV_K ** -0.5),
        'conv_b': nrm((L, 2 * M_HEADS * M_QK), 0.01),
        'i_bias': nrm((L, M_HEADS), 0.1),
        'f_bias': uni((L, M_HEADS), 3.0, 6.0),
        'mh_w': 1.0 + nrm((L, M_WIDTH), 0.05),
        'b_gate': nrm((L, GATE_COLS), 0.01),
        'w_br': nrm((L, R_WIDTH, D), BETA * R_WIDTH ** -0.5),
        'w_bm': nrm((L, M_WIDTH, D), BETA * M_WIDTH ** -0.5),
        'w_out': nrm((L, D, D), BETA * D ** -0.5),
        'ln1_w': 1.0 + nrm((L, D), 0.05),
        'ln1_b': nrm((L, D), 0.01),
        'w_rg': nrm((L, D, N_GROUPS), D ** -0.5),
        'b_rg': nrm((L, N_GROUPS), 0.01),
        'w_re': nrm((L, D, N_EXPERTS), D ** -0.5),
        'b_re': nrm((L, N_EXPERTS), 0.01),
        'w_gate': nrm((L, N_EXPERTS, D, D_EXPERT), BETA * D ** -0.5),
        'w_up': nrm((L, N_EXPERTS, D, D_EXPERT), BETA * D ** -0.5),
        'w_down': nrm((L, N_EXPERTS, D_EXPERT, D), BETA * D_EXPERT ** -0.5),
        'w_pg': nrm((L, D, D), D ** -0.5),
        'w_ple': nrm((L, PLE_DIM, D), BETA * PLE_DIM ** -0.5),
        'ln2_w': 1.0 + nrm((L, D), 0.05),
        'ln2_b': nrm((L, D), 0.01),
    }

def first_block(x, p, w_in, mu_shift, w0, w_w2, a0, w_a2, w_g2, k_k, k_a, r_k, lnx_w, lnx_b,
              conv_w, conv_b, i_bias, f_bias, mh_w, b_gate, w_br, w_bm, w_out, ln1_w, ln1_b,
              w_rg, b_rg, w_re, b_re, w_gate, w_up, w_down, w_pg, w_ple, ln2_w, ln2_b):
    bsz, seq, d = x.shape
    for i in range(DEPTH):
        u = x @ w_in[i]
        u_r, u_m, u_g = _split(u, [RWKV_COLS, MLSTM_COLS, GATE_COLS])
        y_r = _rwkv7_mixer(u_r, mu_shift[i], w0[i], w_w2[i], a0[i], w_a2[i], w_g2[i],
                           k_k[i], k_a[i], r_k[i], lnx_w[i], lnx_b[i])
        y_m = _mlstm_mixer(u_m, conv_w[i], conv_b[i], i_bias[i], f_bias[i], mh_w[i])
        g_r, g_m = _split(u_g + b_gate[i], [d, d])
        mix = (jax.nn.sigmoid(g_r) * (y_r @ w_br[i])
               + jax.nn.sigmoid(g_m) * (y_m @ w_bm[i])) @ w_out[i]
        x = _layer_norm(ALPHA * x + mix, ln1_w[i], ln1_b[i])
        moe = _hier_moe(x.reshape(bsz * seq, d), w_rg[i], b_rg[i], w_re[i], b_re[i],
                        w_gate[i], w_up[i], w_down[i]).reshape(bsz, seq, d)
        ple = jax.nn.sigmoid(x @ w_pg[i]) * (p[i] @ w_ple[i])
        x = _layer_norm(ALPHA * x + moe + ple, ln2_w[i], ln2_b[i])
    return x


DEPTH_2 = 2

CHUNK_2 = 64
N_LEFT_CHUNKS = 8
BAND = (N_LEFT_CHUNKS + 1) * CHUNK_2

A_HEADS = 16
A_HEAD_DIM = 64
A_WIDTH = A_HEADS * A_HEAD_DIM
MAX_REL = 128
N_REL = 2 * MAX_REL + 1

S5_WIDTH = D_MODEL // 2
S5_GROUP = 16
S5_GROUPS = S5_WIDTH // S5_GROUP
S5_STATE = 64
DT_MIN = 0.001
DT_MAX = 0.1

C_HEADS = 16
C_HEAD_DIM = 128
C_WIDTH = C_HEADS * C_HEAD_DIM
Q_BLOCK = 128

EVEN_MIX = A_WIDTH + S5_WIDTH
W_IN_EVEN = 3 * A_WIDTH + S5_WIDTH + A_WIDTH + S5_WIDTH
W_IN_ODD = 3 * C_WIDTH + C_WIDTH + C_HEADS
N_EVEN = (DEPTH_2 + 1) // 2
N_ODD = DEPTH_2 // 2
EPS = 1e-6


def rmsnorm(x, g):
    xf = x.astype(jnp.float32)
    y = xf * lax.rsqrt(jnp.mean(xf * xf, axis=-1, keepdims=True) + EPS)
    return (y * g.astype(jnp.float32)).astype(x.dtype)

def chunked_relpos_attention(q, k, v, rel_bias):
    b, l, h, dh = q.shape
    nc = l // CHUNK_2
    qc = q.reshape(b, nc, CHUNK_2, h, dh)
    pad = ((0, 0), (N_LEFT_CHUNKS, 0), (0, 0), (0, 0), (0, 0))
    kc = jnp.pad(k.reshape(b, nc, CHUNK_2, h, dh), pad)
    vc = jnp.pad(v.reshape(b, nc, CHUNK_2, h, dh), pad)
    band_idx = jnp.arange(nc)[:, None] + jnp.arange(N_LEFT_CHUNKS + 1)[None, :]
    kb = jnp.take(kc, band_idx, axis=1).reshape(b, nc, BAND, h, dh)
    vb = jnp.take(vc, band_idx, axis=1).reshape(b, nc, BAND, h, dh)
    scale = 1.0 / math.sqrt(dh)
    s = jnp.einsum('bcqhd,bckhd->bhcqk', qc, kb).astype(jnp.float32) * scale
    rel = jnp.arange(CHUNK_2)[:, None] + N_LEFT_CHUNKS * CHUNK_2 - jnp.arange(BAND)[None, :]
    rel_idx = jnp.clip(rel, -MAX_REL, MAX_REL) + MAX_REL
    bias = rel_bias.astype(jnp.float32)[:, rel_idx]
    key_chunk = jnp.arange(nc)[:, None] - N_LEFT_CHUNKS + jnp.arange(BAND)[None, :] // CHUNK_2
    valid = key_chunk >= 0
    s = s + bias[None, :, None]
    s = jnp.where(valid[None, None, :, None, :], s, -jnp.inf)
    p = jax.nn.softmax(s, axis=-1).astype(v.dtype)
    o = jnp.einsum('bhcqk,bckhd->bcqhd', p, vb)
    return o.reshape(b, l, h * dh)

def s5_ssm(u, lam_re, lam_im, log_dt, b_re, b_im, c_re, c_im, d_skip):
    bsz, l, _ = u.shape
    uf = u.astype(jnp.float32).reshape(bsz, l, S5_GROUPS, S5_GROUP)
    lr = lam_re.astype(jnp.float32)
    li = lam_im.astype(jnp.float32)
    dt = jnp.exp(log_dt.astype(jnp.float32))[:, None]
    mag = jnp.exp(lr * dt)
    ang = li * dt
    a_re = mag * jnp.cos(ang)
    a_im = mag * jnp.sin(ang)
    den = lr * lr + li * li
    nr = a_re - 1.0
    ni = a_im
    coef_re = (nr * lr + ni * li) / den
    coef_im = (ni * lr - nr * li) / den
    br = b_re.astype(jnp.float32)
    bi = b_im.astype(jnp.float32)
    bb_re = coef_re[..., None] * br - coef_im[..., None] * bi
    bb_im = coef_re[..., None] * bi + coef_im[..., None] * br
    bu_re = jnp.einsum('blgc,gpc->blgp', uf, bb_re)
    bu_im = jnp.einsum('blgc,gpc->blgp', uf, bb_im)
    a_re_t = jnp.broadcast_to(a_re, (1, l, S5_GROUPS, S5_STATE))
    a_im_t = jnp.broadcast_to(a_im, (1, l, S5_GROUPS, S5_STATE))

    def combine(e1, e2):
        ar1, ai1, xr1, xi1 = e1
        ar2, ai2, xr2, xi2 = e2
        return (ar2 * ar1 - ai2 * ai1,
                ar2 * ai1 + ai2 * ar1,
                ar2 * xr1 - ai2 * xi1 + xr2,
                ar2 * xi1 + ai2 * xr1 + xi2)

    _, _, xr, xi = lax.associative_scan(combine, (a_re_t, a_im_t, bu_re, bu_im), axis=1)
    y = (jnp.einsum('blgp,gcp->blgc', xr, c_re.astype(jnp.float32))
         - jnp.einsum('blgp,gcp->blgc', xi, c_im.astype(jnp.float32))
         + d_skip.astype(jnp.float32) * uf)
    return y.reshape(bsz, l, S5_WIDTH)

def forgetting_attention(q, k, v, log_f):
    b, l, h, dh = q.shape
    nqb = l // Q_BLOCK
    cum = jnp.cumsum(log_f, axis=1).transpose(0, 2, 1)
    qb = q.reshape(b, nqb, Q_BLOCK, h, dh).transpose(1, 0, 3, 2, 4)
    cq = cum.reshape(b, h, nqb, Q_BLOCK).transpose(2, 0, 1, 3)
    kpos = jnp.arange(l)
    scale = 1.0 / math.sqrt(dh)

    def block(args):
        qi, cqi, bi = args
        s = jnp.einsum('bhqd,bkhd->bhqk', qi, k).astype(jnp.float32) * scale
        s = s + cqi[..., None] - cum[:, :, None, :]
        qpos = bi * Q_BLOCK + jnp.arange(Q_BLOCK)
        s = jnp.where(kpos[None, :] <= qpos[:, None], s, -jnp.inf)
        p = jax.nn.softmax(s, axis=-1).astype(v.dtype)
        return jnp.einsum('bhqk,bkhd->bqhd', p, v)

    o = lax.map(block, (qb, cq, jnp.arange(nqb)))
    return o.transpose(1, 0, 2, 3, 4).reshape(b, l, h * dh)

def even_layer(x, norm_g, w_in, rel_bias, lam_re, lam_im, log_dt, b_re, b_im,
               c_re, c_im, d_skip, w_glu, b_glu, w_out):
    bsz, l, _ = x.shape
    hn = rmsnorm(x, norm_g)
    proj = hn @ w_in
    cuts = [A_WIDTH, 2 * A_WIDTH, 3 * A_WIDTH, 3 * A_WIDTH + S5_WIDTH,
            4 * A_WIDTH + S5_WIDTH]
    q, k, v, u, z_a, z_b = jnp.split(proj, cuts, axis=-1)
    shp = (bsz, l, A_HEADS, A_HEAD_DIM)
    o_a = chunked_relpos_attention(q.reshape(shp), k.reshape(shp), v.reshape(shp), rel_bias)
    o_a = o_a * jax.nn.silu(z_a)
    y = jax.nn.gelu(s5_ssm(u, lam_re, lam_im, log_dt, b_re, b_im, c_re, c_im, d_skip).astype(x.dtype))
    o_b = y * jax.nn.sigmoid(y @ w_glu + b_glu)
    o_b = o_b * jax.nn.silu(z_b)
    return x + jnp.concatenate([o_a, o_b], axis=-1) @ w_out

def odd_layer(x, norm_g, w_in, b_forget, w_out):
    bsz, l, _ = x.shape
    hn = rmsnorm(x, norm_g)
    proj = hn @ w_in
    cuts = [C_WIDTH, 2 * C_WIDTH, 3 * C_WIDTH, 4 * C_WIDTH]
    q, k, v, z, f_logit = jnp.split(proj, cuts, axis=-1)
    log_f = jax.nn.log_sigmoid((f_logit + b_forget).astype(jnp.float32))
    shp = (bsz, l, C_HEADS, C_HEAD_DIM)
    o = forgetting_attention(q.reshape(shp), k.reshape(shp), v.reshape(shp), log_f)
    o = o * jax.nn.silu(z)
    return x + o @ w_out

def second_inputs(seed: int = 0) -> dict:
    key = jax.random.key(seed)
    ks = jax.random.split(key, 20)
    f32 = jnp.float32
    x = jax.random.normal(ks[0], (BATCH, SEQ, D_MODEL), f32)
    norm_even_g = 1.0 + 0.05 * jax.random.normal(ks[1], (N_EVEN, D_MODEL), f32)
    w_in_even = jax.random.normal(ks[2], (N_EVEN, D_MODEL, W_IN_EVEN), f32) * D_MODEL ** -0.5
    rel_bias = 0.2 * jax.random.normal(ks[3], (N_EVEN, A_HEADS, N_REL), f32)
    n = jnp.arange(S5_STATE, dtype=f32)
    s5_lambda_re = -0.5 + 0.01 * jax.random.normal(ks[4], (N_EVEN, S5_GROUPS, S5_STATE), f32)
    s5_lambda_im = math.pi * n + 0.01 * jax.random.normal(ks[5], (N_EVEN, S5_GROUPS, S5_STATE), f32)
    s5_log_dt = jax.random.uniform(ks[6], (N_EVEN, S5_GROUPS), f32,
                                   math.log(DT_MIN), math.log(DT_MAX))
    s5_b_re = jax.random.normal(ks[7], (N_EVEN, S5_GROUPS, S5_STATE, S5_GROUP), f32) * (2 * S5_GROUP) ** -0.5
    s5_b_im = jax.random.normal(ks[8], (N_EVEN, S5_GROUPS, S5_STATE, S5_GROUP), f32) * (2 * S5_GROUP) ** -0.5
    s5_c_re = jax.random.normal(ks[9], (N_EVEN, S5_GROUPS, S5_GROUP, S5_STATE), f32) * (2 * S5_STATE) ** -0.5
    s5_c_im = jax.random.normal(ks[10], (N_EVEN, S5_GROUPS, S5_GROUP, S5_STATE), f32) * (2 * S5_STATE) ** -0.5
    s5_d = 0.5 * jax.random.normal(ks[11], (N_EVEN, S5_GROUPS, S5_GROUP), f32)
    w_glu = jax.random.normal(ks[12], (N_EVEN, S5_WIDTH, S5_WIDTH), f32) * S5_WIDTH ** -0.5
    b_glu = 0.02 * jax.random.normal(ks[13], (N_EVEN, S5_WIDTH), f32)
    w_out_even = jax.random.normal(ks[14], (N_EVEN, EVEN_MIX, D_MODEL), f32) * EVEN_MIX ** -0.5
    norm_odd_g = 1.0 + 0.05 * jax.random.normal(ks[15], (N_ODD, D_MODEL), f32)
    w_in_odd = jax.random.normal(ks[16], (N_ODD, D_MODEL, W_IN_ODD), f32) * D_MODEL ** -0.5
    b_forget = jax.random.uniform(ks[17], (N_ODD, C_HEADS), f32, 1.0, 4.0)
    w_out_odd = jax.random.normal(ks[18], (N_ODD, C_WIDTH, D_MODEL), f32) * C_WIDTH ** -0.5
    final_norm_g = 1.0 + 0.05 * jax.random.normal(ks[19], (D_MODEL,), f32)
    return {"x": x, "norm_even_g": norm_even_g, "w_in_even": w_in_even, "rel_bias": rel_bias,
            "s5_lambda_re": s5_lambda_re, "s5_lambda_im": s5_lambda_im, "s5_log_dt": s5_log_dt,
            "s5_b_re": s5_b_re, "s5_b_im": s5_b_im, "s5_c_re": s5_c_re, "s5_c_im": s5_c_im,
            "s5_d": s5_d, "w_glu": w_glu, "b_glu": b_glu, "w_out_even": w_out_even,
            "norm_odd_g": norm_odd_g, "w_in_odd": w_in_odd, "b_forget": b_forget,
            "w_out_odd": w_out_odd, "final_norm_g": final_norm_g}

def second_block(x, norm_even_g, w_in_even, rel_bias, s5_lambda_re, s5_lambda_im, s5_log_dt,
              s5_b_re, s5_b_im, s5_c_re, s5_c_im, s5_d, w_glu, b_glu, w_out_even,
              norm_odd_g, w_in_odd, b_forget, w_out_odd, final_norm_g):
    for layer in range(DEPTH_2):
        i = layer // 2
        if layer % 2 == 0:
            x = even_layer(x, norm_even_g[i], w_in_even[i], rel_bias[i], s5_lambda_re[i],
                           s5_lambda_im[i], s5_log_dt[i], s5_b_re[i], s5_b_im[i], s5_c_re[i],
                           s5_c_im[i], s5_d[i], w_glu[i], b_glu[i], w_out_even[i])
        else:
            x = odd_layer(x, norm_odd_g[i], w_in_odd[i], b_forget[i], w_out_odd[i])
    return rmsnorm(x, final_norm_g)


def setup_inputs(seed=0):
    out = dict(first_inputs(seed))
    for name, value in second_inputs(seed + 1).items():
        if name != "x":
            out[name + "_2"] = value
    return out


def reference(
    x, p, w_in, mu_shift, w0, w_w2, a0, w_a2, w_g2, k_k, k_a, r_k, lnx_w, lnx_b, conv_w, conv_b,
    i_bias, f_bias, mh_w, b_gate, w_br, w_bm, w_out, ln1_w, ln1_b, w_rg, b_rg, w_re, b_re,
    w_gate, w_up, w_down, w_pg, w_ple, ln2_w, ln2_b, norm_even_g_2, w_in_even_2, rel_bias_2,
    s5_lambda_re_2, s5_lambda_im_2, s5_log_dt_2, s5_b_re_2, s5_b_im_2, s5_c_re_2, s5_c_im_2,
    s5_d_2, w_glu_2, b_glu_2, w_out_even_2, norm_odd_g_2, w_in_odd_2, b_forget_2, w_out_odd_2,
    final_norm_g_2,
):
    x = first_block(
        x, p, w_in, mu_shift, w0, w_w2, a0, w_a2, w_g2, k_k, k_a, r_k, lnx_w, lnx_b, conv_w,
        conv_b, i_bias, f_bias, mh_w, b_gate, w_br, w_bm, w_out, ln1_w, ln1_b, w_rg, b_rg, w_re,
        b_re, w_gate, w_up, w_down, w_pg, w_ple, ln2_w, ln2_b,
    )
    return second_block(
        x, norm_even_g_2, w_in_even_2, rel_bias_2, s5_lambda_re_2, s5_lambda_im_2, s5_log_dt_2,
        s5_b_re_2, s5_b_im_2, s5_c_re_2, s5_c_im_2, s5_d_2, w_glu_2, b_glu_2, w_out_even_2,
        norm_odd_g_2, w_in_odd_2, b_forget_2, w_out_odd_2, final_norm_g_2,
    )


_drawn_inputs = setup_inputs


def setup_inputs(seed=0):
    import zlib

    import numpy as np

    out = dict(_drawn_inputs(seed))
    spreads = {}
    factors = {'w_w2': 8.0,
     'a0': 8.0,
     'w_a2': 3.093,
     'k_k': 8.0,
     'k_a': 8.0,
     'r_k': 4.726,
     'lnx_w': 8.0,
     'lnx_b': 8.0,
     'conv_b': 8.0,
     'i_bias': 55.023,
     'f_bias': 34.712,
     'mh_w': 8.0,
     'b_gate': 8.0,
     'ln1_b': 4.366,
     'b_rg': 8.0,
     'b_re': 8.0,
     'ln2_b': 4.585,
     'norm_even_g_2': 6.531,
     'rel_bias_2': 4.551,
     's5_lambda_re_2': 64.0,
     's5_lambda_im_2': 58.488,
     's5_log_dt_2': 61.32,
     's5_b_re_2': 64.0,
     's5_b_im_2': 64.0,
     's5_c_re_2': 64.0,
     's5_c_im_2': 64.0,
     'w_glu_2': 4.812,
     'b_glu_2': 64.0,
     'norm_odd_g_2': 2.888}
    for name, (base, spread) in spreads.items():
        noise = np.random.default_rng([zlib.crc32(name.encode()), seed]).standard_normal(out[name].shape)
        drawn = base * np.exp(spread * noise) if base else spread * noise
        out[name] = __import__('jax').numpy.asarray(drawn.astype(out[name].dtype))
    for name, factor in factors.items():
        out[name] = (out[name] * factor).astype(out[name].dtype)
    return out
```

```python
import math

import concourse.bass as bass
from concourse import mybir

F32 = mybir.dt.float32
ALU = mybir.AluOpType
ACT = mybir.ActivationFunctionType
AX = mybir.AxisListType
RING = 5
ALPHA = 2.0 ** 0.25
NEG = -1e30


class Prog:

    def __init__(self, nc, ctx):
        self.nc = nc
        self.ctx = ctx
        self.q = {e: [] for e in ("pe", "dve", "act", "pool", "sp")}
        self.n = {e: 0 for e in self.q}
        self.sem = {e: ctx.enter_context(nc.semaphore("s_" + e)) for e in self.q}
        self.pending = {e: [] for e in self.q}
        self.dma_open = []
        self.nb = 0
        self.slot_sem = [ctx.enter_context(nc.semaphore(f"s_slot{i}")) for i in range(RING)]
        self.slot_free = [None] * RING
        self.pieces = 0
        self.pair_i = 0
        self.pair_free = [()] * 4
        self.pe_signed = True

    def put(self, e, fn, after, sig):
        waits = [t for t in self.pending[e] + list(after) if t is not None]
        self.pending[e] = []
        if sig:
            self.n[e] += 1
        self.q[e].append((fn, waits, (self.sem[e], 1) if sig else None))
        return (self.sem[e], self.n[e]) if sig else None

    def last(self, e):
        return (self.sem[e], self.n[e])

    def pe(self, fn, *after, sig=False):
        self.pe_signed = sig
        return self.put("pe", fn, after, sig)

    def dve(self, fn, *after):
        return self.put("dve", fn, (self.last("dve"),) + after, True)

    def act(self, fn, *after):
        return self.put("act", fn, (self.last("act"),) + after, True)

    def pool(self, fn, *after):
        return self.put("pool", fn, (self.last("pool"),) + after, True)

    def loads(self, pairs, *after, e="pool"):
        s = self.ctx.enter_context(self.nc.semaphore(f"s_dma{self.nb}"))
        self.nb += 1
        waits = [t for t in self.pending[e] + list(after) if t is not None]
        self.pending[e] = []
        for i, (out, in_) in enumerate(pairs):
            self.q[e].append((lambda g, out=out, in_=in_: g.dma_start(out, in_), waits if i == 0 else [], (s, 16)))
        t = (s, 16 * len(pairs))
        self.dma_open.append(t)
        return t

    def barrier(self):
        assert self.pe_signed
        toks = [self.last(e) for e in ("pe", "dve", "act", "pool")] + self.dma_open
        self.dma_open = []
        for e in ("pe", "dve", "act", "pool"):
            self.pending[e] = self.pending[e] + toks

    def emit(self, e, eng):
        seen = {}
        for fn, waits, inc in self.q[e]:
            need = {}
            for s, v in waits:
                k = id(s)
                if v > seen.get(k, (0, 0))[0] and v > need.get(k, (None, 0))[1]:
                    need[k] = (s, v)
            for k, (s, v) in need.items():
                eng.wait_ge(s, v)
                seen[k] = (v, 0)
            if fn is None:
                continue
            ins = fn(eng)
            if inc:
                ins.then_inc(inc[0], inc[1])


def bcast(ap, shape):
    return ap.broadcast_to(shape)


def build(nc, I, out):
    from contextlib import ExitStack

    with ExitStack() as ctx:
        P = Prog(nc, ctx)
        TOT = 53200
        big = ctx.enter_context(nc.sbuf_tensor("big", [128, TOT], F32))
        psum = ctx.enter_context(nc.psum_tensor("psum", [128, 4096], F32))
        top = [0]

        def alloc(n):
            o = top[0]
            top[0] += n
            assert top[0] <= TOT, top[0]
            return big[:, o:o + n]

        def tm(c):
            return alloc(2 * c).rearrange("p (b c) -> p b c", b=2)

        def fm(k):
            return alloc(k * 256).rearrange("p (k t) -> p k t", t=256)

        ring = [alloc(2048) for _ in range(RING)]

        def pair():
            i = P.pair_i
            P.pair_i = (i + 1) % 4
            assert P.pair_free[i] is not None
            free = P.pair_free[i]
            P.pair_free[i] = None
            return i, psum[:, 1024 * i:1024 * i + 1024], free

        def done(i, *toks):
            P.pair_free[i] = toks

        def piece(view, kt, n, rows=128):
            s = P.pieces % RING
            dst = ring[s].rearrange("p (k n) -> p k n", k=4)[0:rows, 0:kt, 0:n]
            sem = P.slot_sem[s]
            free = P.slot_free[s]
            P.q["sp"].append((lambda g: g.dma_start(dst, view), [free] if free else [], (sem, 16)))
            tok = (sem, 16 * (P.pieces // RING + 1))
            P.pieces += 1
            return s, dst, tok

        def finish():
            with nc.Block() as block:
                @block.sync
                def _(e):
                    P.emit("sp", e)

                @block.tensor
                def _(e):
                    P.emit("pe", e)

                @block.vector
                def _(e):
                    P.emit("dve", e)

                @block.scalar
                def _(e):
                    P.emit("act", e)

                @block.gpsimd
                def _(e):
                    P.emit("pool", e)

        ident = alloc(128)
        shiftd = alloc(128)
        carry = alloc(128)
        ucent = alloc(128)
        tri_inc = alloc(128)
        tri_str = alloc(128)
        invm = alloc(7 * 128).rearrange("p (l t) -> p l t", l=7)
        cmask = alloc(128)
        ones = alloc(512)
        cols = alloc(4)
        sel = alloc(16 * 128).rearrange("p (h t) -> p h t", h=16)
        CD = math.exp(-0.5)

        def asel(o, i, op, fill, base, pattern, cm):
            return P.pool(lambda g: g.affine_select(out=o, in_=i, compare_op=op, fill=fill, base=base,
                                                    pattern=pattern, channel_multiplier=cm))

        P.pool(lambda g: g.memset(ones, 1.0))
        one = ones[:, 0:128]
        P.pool(lambda g: g.memset(ident, 0.0))
        asel(ident, ident, ALU.not_equal, 1.0, 0, [[-1, 128]], 1)
        P.pool(lambda g: g.memset(shiftd, 0.0))
        asel(shiftd, shiftd, ALU.not_equal, 1.0, 1, [[-1, 128]], 1)
        asel(shiftd, shiftd, ALU.not_equal, -1.0, 0, [[-1, 128]], 1)
        P.pool(lambda g: g.memset(carry, 0.0))
        asel(carry, carry, ALU.not_equal, 1.0, -127, [[128, 128]], 1)
        asel(tri_inc, one, ALU.is_ge, 0.0, 0, [[1, 128]], -1)
        asel(tri_str, one, ALU.is_gt, 0.0, 0, [[1, 128]], -1)
        P.pool(lambda g: g.memset(ucent, -CD))
        asel(ucent, ucent, ALU.is_ge, 0.0, 0, [[1, 128]], -1)
        t_c = P.pool(lambda g: g.tensor_scalar(ucent[0:64, :], ucent[0:64, :], CD, None, ALU.add))
        for l in range(7):
            b = 1 << l
            m = invm[:, l, :]
            P.pool(lambda g, m=m: g.memset(m, 0.0))
            v = m.rearrange("p (n h r) -> p n h r", h=2, r=b)[:, :, 1, :]
            o1 = ones[:, 0:64].rearrange("p (n r) -> p n r", r=b)
            asel(v, o1, ALU.is_ge, 0.0, 0, [[-2 * b, 64 // b], [0, b]], 1)
            asel(v, v, ALU.is_gt, 0.0, b, [[2 * b, 64 // b], [0, b]], -1)
        P.pool(lambda g: g.memset(cmask, 0.0))
        asel(cmask, cmask, ALU.is_ge, NEG, 0, [[-1, 128]], 1)
        P.pool(lambda g: g.memset(cols, -CD))
        asel(cols[:, 0:1], cols[:, 0:1], ALU.is_gt, 0.0, -63, [[0, 1]], 1)
        asel(cols[:, 1:2], cols[:, 1:2], ALU.is_gt, 0.0, 64, [[0, 1]], -1)
        P.pool(lambda g: g.memset(cols[:, 2:3], 0.0))
        P.pool(lambda g: g.memset(sel, 0.0))
        t_const = asel(sel, sel, ALU.not_equal, 1.0, 0, [[-1, 16], [0, 128]], 1)

        x = tm(2048)
        mark_x = top[0]
        t_x = P.loads([(x, I["x"][0].rearrange("(b p) d -> p b d", p=128))], e="act")

        def copy(e, o, i, *after, scale=None):
            if e == "act":
                return P.act(lambda g: g.activation(o, i, ACT.Copy, scale=1.0 if scale is None else scale), *after)
            if scale is None:
                return P.dve(lambda g: g.tensor_copy(o, i), *after)
            return P.dve(lambda g: g.tensor_scalar(o, i, scale, None, ALU.mult), *after)

        def rcp(o, i, *after):
            return P.dve(lambda g: g.reciprocal(o, i), *after)

        def mset(o, value):
            return P.dve(lambda g: g.memset(o, value))

        def tt(o, a, b, op, *after):
            return P.dve(lambda g: g.tensor_tensor(o, a, b, op), *after)

        def ts(o, a, s1, s2, o1, o2=None, *after):
            if o2 is None:
                return P.dve(lambda g: g.tensor_scalar(o, a, s1, None, o1), *after)
            return P.dve(lambda g: g.tensor_scalar(o, a, s1, s2, o1, o2), *after)

        def stt(o, a, s, b, o1, o2, *after):
            return P.dve(lambda g: g.scalar_tensor_tensor(out=o, in0=a, scalar=s, in1=b, op0=o1, op1=o2), *after)

        def actf(o, i, f, *after, bias=None, scale=1.0):
            if bias is None:
                return P.act(lambda g: g.activation(o, i, f, scale=scale), *after)
            return P.act(lambda g: g.activation(o, i, f, bias=bias, scale=scale), *after)

        def red(o, i, op, *after):
            return P.dve(lambda g: g.tensor_reduce(o, i, AX.X, op), *after)

        def mm(o, l, r, start, stop, *after, sig=False):
            return P.pe(lambda g: g.matmul(o, l, r, start=start, stop=stop, skip_group_check=True), *after, sig=sig)

        def tr(o, i, *after, sig=False):
            k = i.shape[0]
            return P.pe(lambda g: g.transpose(o, i, ident[0:k, 0:k]), *after, sig=sig)

        def to_fm(src, dst, C, *after):
            toks = [None, None]
            for j in range(C // 512):
                i, ps, free = pair()
                v = ps.rearrange("p (b k t) -> p b k t", b=2, k=4)
                for b in range(2):
                    for k in range(4):
                        t = tr(v[:, b, k, :], src[:, b, 512 * j + 128 * k:512 * j + 128 * k + 128],
                               *((free + after) if b == 0 and k == 0 else ()), sig=(b == 1 and k == 3))
                d = dst[:, 4 * j:4 * j + 4, :].rearrange("p k (b t) -> p b k t", b=2)
                toks[j % 2] = copy("act" if j % 2 else "dve", d, v, t)
                done(i, toks[j % 2])
            return tuple(t for t in toks if t)

        def proj_a(xT, KT, w, c0, ncols, consume, *after, bias=None):
            for ci, c in enumerate(range(0, ncols, 512)):
                n = min(512, ncols - c)
                i, ps, free = pair()
                v = ps.rearrange("p (b n) -> p b n", b=2)[:, :, 0:n]
                first = free + after
                if bias is not None:
                    for b in range(2):
                        mm(v[:, b, :], ones[0:1, 0:128], bias[0:1, c:c + n], True, False, *first)
                        first = ()
                for g0 in range(0, KT, 4):
                    kn = min(4, KT - g0)
                    s, sl, tok = piece(w[128 * g0:128 * (g0 + kn), c0 + c:c0 + c + n].rearrange(
                        "(k p) n -> p k n", p=128), kn, n)
                    for b in range(2):
                        for k in range(kn):
                            t = mm(v[:, b, :], xT[:, g0 + k, 128 * b:128 * b + 128], sl[:, k, :],
                                   bias is None and g0 + k == 0, g0 + k == KT - 1, tok, *first,
                                   sig=(b == 1 and k == kn - 1))
                            first = ()
                    P.slot_free[s] = t
                done(i, *consume(ci, n, v, t))

        def proj_b(xT, KT, w, c0, ncols, consume, *after):
            for ci in range(ncols // 512):
                c = c0 + 512 * ci
                i, ps, free = pair()
                v = ps.rearrange("p (m t) -> p m t", m=4)
                first = free + after
                for g0 in range(0, KT, 4):
                    kn = min(4, KT - g0)
                    s, sl, tok = piece(w[128 * g0:128 * (g0 + kn), c:c + 512].rearrange(
                        "(k p) n -> p k n", p=128), kn, 512)
                    for m in range(4):
                        for k in range(kn):
                            t = mm(v[:, m, :], sl[:, k, 128 * m:128 * m + 128], xT[:, g0 + k, :],
                                   g0 + k == 0 and m % 2 == 0, g0 + k == KT - 1, tok, *first,
                                   sig=(m == 3 and k == kn - 1))
                            first = ()
                    P.slot_free[s] = t
                done(i, *consume(ci, v, t))

        def dump(v, *after):
            o = out[0].rearrange("(b p) d -> p b d", p=128)
            t = P.loads([(o[:, :, 0:v.shape[2]], v)], *after, e="act")
            P.q["act"].append((None, [t], None))
            finish()

        xT = fm(16)
        t_xT = to_fm(x, xT, 2048, t_x, t_const)
        mark0 = top[0]
        W = I["w_in"][0]

        P.barrier()
        UR = tm(3360)
        A1, A2 = [x.rearrange("p b c -> p (b c)")[:, 2048 * k:2048 * k + 2048].rearrange("p (b c) -> p b c", b=2)
                  for k in range(2)]
        A3 = tm(1024)
        PB, QB, RB, BB = tm(1024), tm(1024), tm(1024), tm(1024)
        fmbase = top[0]
        turned = alloc(2048)
        aT, bT, cT, rT = [turned[:, 512 * k:512 * k + 512].rearrange("p (q t) -> p q t", q=4) for k in range(4)]
        mats = top[0]
        LT, X, XT, T1, LB = [alloc(1024).rearrange("p (h t) -> p h t", h=8) for _ in range(5)]
        loraT = alloc(1280).rearrange("p (k t) -> p k t", t=256)
        nmv, nu, nh, nht = [alloc(512) for _ in range(4)]
        small = alloc(256)
        kstate = alloc(8 * 64).rearrange("p (i v) -> p i v", i=8)
        pz = alloc(8)
        mub = big[:, fmbase:fmbase + 3360]
        par = big[:, fmbase + 3360:fmbase + 6432].rearrange("p (k c) -> p k c", k=3)
        rows = big[0:1, mats + 5120 + 1280:mats + 5120 + 1280 + 2048]
        t_mu = P.loads([(mub, I["mu_shift"][0].partition_broadcast(128)),
                        (par[:, 0, :], I["k_k"][0].partition_broadcast(128)),
                        (par[:, 1, :], I["k_a"][0].partition_broadcast(128)),
                        (par[:, 2, :], I["r_k"][0].rearrange("h n -> (h n)").partition_broadcast(128)),
                        (rows[:, 0:1024], I["w0"]), (rows[:, 1024:2048], I["a0"])])

        def eat_ur(ci, n, ps, t):
            d = UR[:, :, 512 * ci:512 * ci + n]
            t1 = copy("act", d, ps, t)
            i, p2, free = pair()
            v = p2.rearrange("p (b n) -> p b n", b=2)[:, :, 0:n]
            mm(v[:, 0, :], shiftd, d[:, 0, :], True, True, t1, *free)
            mm(v[:, 1, :], shiftd, d[:, 1, :], True, False)
            t2 = mm(v[:, 1, :], carry, d[:, 0, :], False, True, sig=True)
            mb = mub[:, 512 * ci:512 * ci + n].unsqueeze(1).broadcast_to([128, 2, n])
            t3 = tt(v, v, mb, ALU.mult, t2, t_mu)
            t4 = tt(d, d, v, ALU.add, t3)
            done(i, t4)
            return (t1,)

        proj_a(xT, 16, W, 0, 3360, eat_ur, *t_xT)
        r_, k_, v_ = [UR[:, :, 1024 * i:1024 * i + 1024] for i in range(3)]
        lo = UR[:, :, 3072:3360]
        t_l = actf(lo[:, :, 0:64], lo[:, :, 0:64], ACT.Tanh, P.last("dve"))
        t_l = actf(lo[:, :, 128:288], lo[:, :, 128:288], ACT.Sigmoid)
        i, ps, free = pair()
        pv = ps.rearrange("p (k t) -> p k t", t=256)
        i2, ps2, free2 = pair()
        pv2 = ps2.rearrange("p (k t) -> p k t", t=256)
        for b in range(2):
            tb = slice(128 * b, 128 * b + 128)
            tr(pv[0:64, 0, tb], lo[:, b, 0:64], t_l, *(free if b == 0 else ()))
            tr(pv[0:64, 1, tb], lo[:, b, 64:128])
            tr(pv[:, 2, tb], lo[:, b, 128:256])
            t = tr(pv2[0:32, 0, tb], lo[:, b, 256:288], *(free2 if b == 0 else ()), sig=True)
        copy("dve", loraT[0:64, 0:2, :], pv[0:64, 0:2, :], t)
        copy("dve", loraT[:, 2, :], pv[:, 2, :])
        t_lT = copy("dve", loraT[0:32, 3, :], pv2[0:32, 0, :])
        done(i, t_lT)
        done(i2, t_lT)

        def lora(wname, row, parts, consume):
            w = I[wname][0]
            sls = []
            r0 = 0
            for (kk_, rr) in parts:
                s, sl, tok = piece(w[r0:r0 + rr, :].rearrange("p (k n) -> p k n", k=2), 2, 512, rows=rr)
                sls.append((s, sl, tok, kk_, rr))
                r0 += rr
            for c in range(2):
                i, ps, free = pair()
                v = ps.rearrange("p (b n) -> p b n", b=2)
                first = free + (t_lT, t_mu)
                for b in range(2):
                    st = True
                    if row is not None:
                        mm(v[:, b, :], ones[0:1, 0:128], row[:, 512 * c:512 * c + 512], True, False, *first)
                        first, st = (), False
                    for j, (s, sl, tok, kk_, rr) in enumerate(sls):
                        t = mm(v[:, b, :], loraT[0:rr, kk_, 128 * b:128 * b + 128], sl[:, c, :], st,
                               j == len(sls) - 1, tok, *first, sig=(b == 1 and j == len(sls) - 1))
                        first, st = (), False
                done(i, consume(c, v, t))
            for s, *_ in sls:
                P.slot_free[s] = t

        sig_ = A1
        lora("w_w2", rows[:, 0:1024], [(0, 64)],
             lambda c, v, t: actf(sig_[:, :, 512 * c:512 * c + 512], v, ACT.Sigmoid, t))
        lora("w_a2", rows[:, 1024:2048], [(1, 64)],
             lambda c, v, t: actf(A2[:, :, 512 * c:512 * c + 512], v, ACT.Sigmoid, t))
        t_sig = P.last("act")
        t_dec = None
        for c in range(2):
            cs = slice(512 * c, 512 * c + 512)
            i, ps, free = pair()
            v = ps.rearrange("p (b n) -> p b n", b=2)
            mm(v[:, 0, :], ucent, sig_[:, 0, cs], True, True, t_sig, *free)
            t = mm(v[:, 1, :], ucent, sig_[:, 1, cs], True, True, sig=True)
            actf(PB[:, :, cs], v, ACT.Exp, t)
            t1 = actf(QB[:, :, cs], v, ACT.Exp, scale=-1.0)
            t2 = stt(v, sig_[:, :, cs], CD, v, ALU.mult, ALU.add, t1)
            t_dec = actf(RB[:, :, cs], v, ACT.Exp, t2)
            done(i, t_dec)
        i, ps, free = pair()
        for j in range(8):
            mm(ps[:, j:j + 1], sig_[:, 0, 128 * j:128 * j + 128], cols[:, 0:1], True, False, *(free if j == 0 else ()))
            t = mm(ps[:, j:j + 1], sig_[:, 1, 128 * j:128 * j + 128], cols[:, 1:2], False, True, sig=(j == 7))
        t_pz = actf(pz, ps[:, 0:8], ACT.Exp, t)
        done(i, t_pz)
        kk = A3

        def hd(v):
            return v.rearrange("p b (h n) -> p b h n", n=64)

        def pb(k):
            return par[:, k, :].unsqueeze(1).broadcast_to([128, 2, 1024])

        sm = small.rearrange("p (k b h) -> p k b h", k=8, b=2)
        tt(kk, k_, pb(0), ALU.mult, t_mu)
        tt(BB, kk, kk, ALU.mult)
        for b in range(2):
            t = red(sm[:, 0, b, :], hd(BB)[:, b], ALU.add)
        t = actf(sm[:, 1], sm[:, 0], ACT.Sqrt, t)
        ts(sm[:, 1], sm[:, 1], 1e-12, None, ALU.max, None, t)
        rcp(sm[:, 2], sm[:, 1])
        for b in range(2):
            rk = sm[:, 2, b, :].unsqueeze(2).broadcast_to([128, 16, 64])
            tt(hd(kk)[:, b], hd(kk)[:, b], rk, ALU.mult)
        aa = A2
        stt(BB, aa, -1.0, pb(1), ALU.add, ALU.mult)
        stt(k_, BB, 1.0, k_, ALU.add, ALU.mult)
        tt(BB, r_, k_, ALU.mult)
        tt(BB, BB, pb(2), ALU.mult)
        for b in range(2):
            red(sm[:, 3, b, :], hd(BB)[:, b], ALU.add)
        tt(BB, aa, kk, ALU.mult)
        tt(BB, BB, QB, ALU.mult, t_dec)
        tt(QB, QB, k_, ALU.mult)
        tt(RB, RB, kk, ALU.mult)
        t_sc = tt(PB, PB, r_, ALU.mult)
        Y = A1
        t_all = P.last("act")
        for b in range(2):
            tb = slice(128 * b, 128 * b + 128)
            for hg in range(2):
                for two in range(2):
                    i, ps, free = pair()
                    for j in range(8):
                        src = (RB, BB, QB, PB)[2 * two + j // 4]
                        t = tr(ps[:, 128 * j:128 * j + 128],
                               src[:, b, 512 * hg + 128 * (j % 4):512 * hg + 128 * (j % 4) + 128],
                               *((t_sc,) + free if j == 0 else ()), sig=(j == 7))
                    t_fm = copy("dve", turned[:, 1024 * two:1024 * two + 1024], ps, t)
                    done(i, t_fm)
                def head(par_, q):
                    return 8 * hg + 2 * q + par_

                def grid(lf, rf, o, after, mask=None, scale=None, e="dve"):
                    i, ps, free = pair()
                    v = ps.rearrange("p (h t) -> p h t", h=8)
                    for par_ in range(2):
                        for q in range(4):
                            j = 4 * par_ + q
                            t = mm(v[:, j, :], lf(par_, q), rf(par_, q), True, True,
                                   *((free + after) if j == 0 else ()), sig=(j == 7))
                    if mask is not None:
                        mb = mask.unsqueeze(1).broadcast_to([128, 8, 128])
                        t = tt(o, v, mb, ALU.mult, t)
                    else:
                        t = copy(e, o, v, t)
                    done(i, t)
                    return t

                def row(T):
                    return lambda par_, q: T[64 * par_:64 * par_ + 64, q, :]

                t_lt = grid(row(bT), row(aT), LT, (t_fm,), mask=tri_str)
                idb = ident.unsqueeze(1).broadcast_to([128, 8, 128])
                copy("dve", X, idb)
                t_xx = copy("dve", XT, idb)
                for l in range(7):
                    mb = invm[:, l, :].unsqueeze(1).broadcast_to([128, 8, 128])
                    t_lb = tt(LB, LT, mb, ALU.mult)
                    t_t1 = grid(lambda a_, q: LB[:, 4 * a_ + q, :], lambda a_, q: X[:, 4 * a_ + q, :], T1,
                                (t_lb, t_xx), e="act")
                    i, ps, free = pair()
                    v = ps.rearrange("p (h t) -> p h t", h=8)
                    i2, ps2, free2 = pair()
                    v2 = ps2.rearrange("p (h t) -> p h t", h=8)
                    for j in range(8):
                        mm(v[:, j, :], XT[:, j, :], T1[:, j, :], True, True, *((t_t1,) + free if j == 0 else ()))
                        t = mm(v2[:, j, :], T1[:, j, :], XT[:, j, :], True, True, *(free2 if j == 0 else ()),
                               sig=(j == 7))
                    t_xx = tt(X, X, v, ALU.subtract, t)
                    done(i, t_xx)
                    t_xx = tt(XT, XT, v2, ALU.subtract)
                    done(i2, t_xx)
                t_m = grid(row(cT), row(aT), T1, (), mask=tri_str)
                t_r1 = grid(row(cT), row(rT), LB, (), mask=tri_inc)
                t_r2 = grid(row(bT), row(rT), LT, (), mask=tri_inc)
                vh = v_[:, b, :].rearrange("p (h n) -> p h n", n=64)
                nmv8, nu8, nh8 = [z.rearrange("p (h n) -> p h n", n=64) for z in (nmv, nu, nh)]
                nht4 = nht.rearrange("p (q t) -> p q t", q=4)

                def grid64(lf, rf, o, after, scale=None, e="dve"):
                    i, ps, free = pair()
                    v = ps[:, 0:512].rearrange("p (h n) -> p h n", h=8)
                    for j in range(8):
                        t = mm(v[:, j, :], lf(j // 4, j % 4), rf(j // 4, j % 4), True, True,
                               *((free + after) if j == 0 else ()), sig=(j == 7))
                    t = copy(e, o, v, t, scale=scale)
                    done(i, t)
                    return t

                t_mv = grid64(lambda a_, q: T1[:, 4 * a_ + q, :], lambda a_, q: vh[:, head(a_, q), :], nmv8,
                              (t_m, P.last("pe")), scale=-1.0)
                t_u = grid64(lambda a_, q: XT[:, 4 * a_ + q, :], lambda a_, q: nmv8[:, 4 * a_ + q, :], nu8, (t_mv,))
                alh = RB[:, b, :].rearrange("p (h n) -> p h n", n=64)
                if b == 1:
                    t_h = grid64(lambda a_, q: XT[:, 4 * a_ + q, :], lambda a_, q: alh[:, head(a_, q), :],
                                 nh.rearrange("p (q a n) -> p a q n", q=4, a=2), (), scale=-1.0)
                    i, ps, free = pair()
                    v = ps[:, 0:512].rearrange("p (q t) -> p q t", q=4)
                    for q in range(4):
                        t = tr(v[:, q, :], nh[:, 128 * q:128 * q + 128], *((t_h,) + free if q == 0 else ()), sig=(q == 3))
                    t_ht = copy("dve", nht4, v, t)
                    done(i, t_ht)
                    i, ps, free = pair()
                    for a_ in range(2):
                        for q in range(4):
                            o = ps[:, 512 * a_ + 64 * q:512 * a_ + 64 * q + 64]
                            t = mm(o, nht4[64 * a_:64 * a_ + 64, q, :], kstate[64 * a_:64 * a_ + 64, 4 * hg + q, :],
                                   True, True, *((t_ht,) + free if a_ + q == 0 else ()), sig=(a_ + q == 4))
                    for a_ in range(2):
                        t_u = tt(nu8[:, 4 * a_:4 * a_ + 4, :], nu8[:, 4 * a_:4 * a_ + 4, :],
                                 ps[:, 512 * a_:512 * a_ + 256].rearrange("p (q n) -> p q n", q=4), ALU.add, t)
                    done(i, t_u)
                i, ps, free = pair()
                first = free + (t_u, t_r1, t_r2)
                for a_ in range(2):
                    for q in range(4):
                        o = ps[:, 512 * a_ + 64 * q:512 * a_ + 64 * q + 64]
                        st = True
                        if b == 1:
                            mm(o, rT[64 * a_:64 * a_ + 64, q, :],
                               kstate[64 * a_:64 * a_ + 64, 4 * hg + q, :], True, False, *first)
                            st, first = False, ()
                        mm(o, LB[:, 4 * a_ + q, :], vh[:, head(a_, q), :], st, False, *first)
                        first = ()
                        t = mm(o, LT[:, 4 * a_ + q, :], nu8[:, 4 * a_ + q, :], False, True, sig=(a_ + q == 4))
                for a_ in range(2):
                    yo = Y[:, b, 512 * hg:512 * hg + 512].rearrange("p (q a n) -> p a q n", q=4, a=2)[:, a_]
                    t_y = copy("dve", yo, ps[:, 512 * a_:512 * a_ + 256].rearrange("p (q n) -> p q n", q=4), t)
                done(i, t_y)
                if b == 0:
                    i, ps, free = pair()
                    kh, bh = [z[:, 0, :].rearrange("p (h n) -> p h n", n=64) for z in (QB, BB)]
                    for a_ in range(2):
                        for q in range(4):
                            o = ps[64 * a_:64 * a_ + 64, 512 * a_ + 64 * q:512 * a_ + 64 * q + 64]
                            mm(o, kh[:, head(a_, q), :], vh[:, head(a_, q), :], True, False,
                               *(free if a_ + q == 0 else ()))
                            t = mm(o, bh[:, head(a_, q), :], nu8[:, 4 * a_ + q, :], False, True, sig=(a_ + q == 4))
                    for a_ in range(2):
                        pa = slice(64 * a_, 64 * a_ + 64)
                        pzb = pz[pa, 4 * hg:4 * hg + 4].unsqueeze(2).broadcast_to([64, 4, 64])
                        t_z = tt(kstate[pa, 4 * hg:4 * hg + 4, :],
                                 ps[pa, 512 * a_:512 * a_ + 256].rearrange("p (q n) -> p q n", q=4),
                                 pzb, ALU.mult, t, t_pz)
                    done(i, t_z)
                P.pending["pe"] = P.pending["pe"] + [P.last("dve")]
        t_ln = P.loads([(A3[:, 0, :], I["lnx_w"][0].partition_broadcast(128)),
                        (A3[:, 1, :], I["lnx_b"][0].partition_broadcast(128))], t_sc)
        G = A2
        lora("w_g2", None, [(2, 128), (3, 32)],
             lambda c, v, t: copy("act", G[:, :, 512 * c:512 * c + 512], v, t, t_sc))
        t_g = P.last("act")

        def head_norm(y, tmp, s, nh_, n, eps):
            yh = y.rearrange("p b (h n) -> p b h n", n=n)
            th = tmp.rearrange("p b (h n) -> p b h n", n=n)
            for b in range(2):
                red(s[:, 0, b, :], yh[:, b], ALU.add)
            ts(s[:, 0], s[:, 0], 1.0 / n, None, ALU.mult)
            for b in range(2):
                tt(yh[:, b], yh[:, b], s[:, 0, b, :].unsqueeze(2).broadcast_to([128, nh_, n]), ALU.subtract)
            tt(tmp, y, y, ALU.mult)
            for b in range(2):
                red(s[:, 1, b, :], th[:, b], ALU.add)
            t = ts(s[:, 1], s[:, 1], 1.0 / n, eps, ALU.mult, ALU.add)
            t = actf(s[:, 2], s[:, 1], ACT.Sqrt, t)
            rcp(s[:, 3], s[:, 2], t)
            for b in range(2):
                tt(yh[:, b], yh[:, b], s[:, 3, b, :].unsqueeze(2).broadcast_to([128, nh_, n]), ALU.mult)

        head_norm(Y, PB, sm[:, 4:8], 16, 64, 64e-5)
        tt(Y, Y, A3[:, 0, :].unsqueeze(1).broadcast_to([128, 2, 1024]), ALU.mult, t_ln)
        tt(Y, Y, A3[:, 1, :].unsqueeze(1).broadcast_to([128, 2, 1024]), ALU.add)
        for b in range(2):
            tt(hd(PB)[:, b], hd(v_)[:, b], sm[:, 3, b, :].unsqueeze(2).broadcast_to([128, 16, 64]), ALU.mult)
        tt(Y, Y, PB, ALU.add)
        t_yr = tt(Y, Y, G, ALU.mult, t_g)
        yrT = big[:, mark0:mark0 + 2048].rearrange("p (k t) -> p k t", t=256)
        P.barrier()
        t_yrT = to_fm(Y, yrT, 1024, t_yr)
        P.barrier()
        top[0] = mark0 + 2048

        qk, qc, qs = fm(8), fm(8), fm(8)
        vm, om, hm, tmp = tm(1024), tm(1024), tm(1024), tm(1024)
        cw = alloc(40).rearrange("p (j k) -> p j k", j=5)
        rw = alloc(8 * 256).rearrange("p (k t) -> p k t", t=256)
        rr = alloc(6 * 128).rearrange("p (b k t) -> p b k t", b=2, k=3)
        gb = alloc(4)
        colz = alloc(48).rearrange("p (b k h) -> p b k h", b=2, k=3)
        E = alloc(1024).rearrange("p (h t) -> p h t", h=8)
        kg = alloc(512)
        cst = alloc(4 * 129).rearrange("p (q v) -> p q v", q=4)
        sm2 = alloc(8 * 16).rearrange("p (k b h) -> p k b h", k=8, b=2)
        mhw = alloc(1024)
        bgr = alloc(4096)
        t_p = P.loads([(cw, I["conv"]), (gb[0:8, 0:1], I["i_bias"].rearrange("o h -> h o")),
                       (gb[0:8, 1:2], I["f_bias"].rearrange("o h -> h o")),
                       (mhw, I["mh_w"][0].partition_broadcast(128)), (bgr[0:1, :], I["b_gate"])])

        proj_b(xT, 16, W, 3360, 1024, lambda ci, v, t: (copy("act", qk[:, 4 * ci:4 * ci + 4, :], v, t),))
        t_qk = P.last("act")
        proj_a(xT, 16, W, 4384, 1024, lambda ci, n, v, t: (copy("act", vm[:, :, 512 * ci:512 * ci + n], v, t),))
        t_v = P.last("act")
        i, ps, free = pair()
        for g0 in range(0, 16, 4):
            s, sl, tok = piece(W[128 * g0:128 * g0 + 512, 5408:5424].rearrange("(k p) n -> p k n", p=128), 4, 16)
            for k in range(4):
                mm(ps[0:8, 0:256], sl[:, k, 0:8], xT[:, g0 + k, :], g0 + k == 0, g0 + k == 15, tok,
                   *(free if g0 + k == 0 else ()))
                t = mm(ps[0:8, 512:768], sl[:, k, 8:16], xT[:, g0 + k, :], g0 + k == 0, g0 + k == 15, sig=(k == 3))
            P.slot_free[s] = t
        R = [rw[0:8, k, :] for k in range(8)]
        ts(R[0], ps[0:8, 0:256], gb[0:8, 0:1], None, ALU.add, None, t, t_p)
        t = ts(R[1], ps[0:8, 512:768], gb[0:8, 1:2], None, ALU.add)
        done(i, t)

        def log_sigmoid(f, s, o, after=()):
            t = stt(s, f, -1.0, f, ALU.mult, ALU.max, *after)
            t = actf(s, s, ACT.Exp, t, scale=-1.0)
            t = actf(s, s, ACT.Ln, bias=ones[0:s.shape[0], 0:1])
            return stt(o, f, 0.0, s, ALU.min, ALU.subtract, t)

        log_sigmoid(R[1], R[2], R[3])
        mset(R[7], 1.0)

        def scan(o, d0, d1, init, o0, o1, *after):
            return P.dve(lambda g: g.tensor_tensor_scan(o, d0, d1, init, o0, o1), *after)

        for b in range(2):
            tb = slice(128 * b, 128 * b + 128)
            scan(R[4][:, tb], R[7][:, tb], R[3][:, tb], 0.0, ALU.mult, ALU.add)
            tt(R[5][:, tb], R[0][:, tb], R[4][:, tb], ALU.subtract)
            if b == 0:
                scan(R[6][:, tb], R[5][:, tb], R[5][:, tb], -3e38, ALU.max, ALU.max)
                tt(gb[0:8, 2:3], R[4][:, 127:128], R[6][:, 127:128], ALU.add)
                ts(gb[0:8, 3:4], R[6][:, 127:128], -1.0, None, ALU.mult)
            else:
                scan(R[6][:, tb], R[5][:, tb], R[5][:, tb], gb[0:8, 2:3], ALU.max, ALU.max)
            copy("dve", rr[0:8, b, 0, :], R[5][:, tb])
            t = tt(rr[0:8, b, 1, :], R[4][:, tb], R[6][:, tb], ALU.add)
            actf(rr[0:8, b, 1, :], rr[0:8, b, 1, :], ACT.Exp, t, scale=-1.0)
            if b == 0:
                t_rr = actf(rr[0:8, 0, 2, :], R[5][:, tb], ACT.Exp, bias=gb[0:8, 3:4])
            else:
                t_rr = actf(rr[0:8, 1, 2, :], R[6][:, tb], ACT.Exp, scale=-1.0, bias=gb[0:8, 2:3])
        i, ps, free = pair()
        for b in range(2):
            for k in range(3):
                t = tr(ps[:, 24 * b + 8 * k:24 * b + 8 * k + 8], rr[0:8, b, k, :],
                       *((t_rr,) + free if b + k == 0 else ()), sig=(b + k == 3))
        t = copy("dve", colz, ps[:, 0:48].rearrange("p (b k h) -> p b k h", b=2, k=3), t)
        done(i, t)
        for j in range(8):
            ts(qc[:, j, :], qk[:, j, :], cw[:, 3, j:j + 1], cw[:, 4, j:j + 1], ALU.mult, ALU.add, t_qk, t_p)
            for d in range(1, 4):
                stt(qc[:, j, d:256], qk[:, j, 0:256 - d], cw[:, 3 - d, j:j + 1], qc[:, j, d:256], ALU.mult, ALU.add)
        t = actf(qs, qc, ACT.Sigmoid, P.last("dve"))
        tt(qs[:, 0:4, :], qs[:, 0:4, :], qc[:, 0:4, :], ALU.mult, t)
        t_qs = stt(qs[:, 4:8, :], qs[:, 4:8, :], 0.125, qc[:, 4:8, :], ALU.mult, ALU.mult)
        proj_a(xT, 16, W, 5424, 1024, lambda ci, n, v, t: (
            actf(om[:, :, 512 * ci:512 * ci + n], v, ACT.Sigmoid, t),))
        t_o = P.last("act")
        vh = vm.rearrange("p b (h n) -> p b h n", n=128)
        hh = hm.rearrange("p b (h n) -> p b h n", n=128)

        def hsel(j):
            return 2 * (j % 4) + j // 4

        for b in range(2):
            tb = slice(128 * b, 128 * b + 128)
            i, ps, free = pair()
            v = ps.rearrange("p (h t) -> p h t", h=8)
            for j in range(8):
                t = mm(v[:, j, :], sel[0:8, hsel(j), :], R[6][:, tb], True, True,
                       *((P.last("dve"),) + free if j == 0 else ()), sig=(j == 7))
            for j in range(8):
                g_ = colz[:, b, 0, hsel(j):hsel(j) + 1]
                t1 = ts(E[:, j, :], v[:, j, :], g_, 0.0, ALU.subtract, ALU.max, t)
            done(i, t1)
            t = actf(E, E, ACT.Exp, t1, scale=-1.0)
            tt(E, E, tri_inc.unsqueeze(1).broadcast_to([128, 8, 128]), ALU.mult, t)
            i, ps, free = pair()
            v = ps.rearrange("p (h t) -> p h t", h=8)
            for j in range(8):
                pa, q = slice(64 * (j // 4), 64 * (j // 4) + 64), j % 4
                t = mm(v[:, j, :], qs[pa, 4 + q, tb], qs[pa, q, tb], True, True,
                       *((t_qs,) + free if j == 0 else ()), sig=(j == 7))
            t_e = tt(E, E, v, ALU.mult, t)
            done(i, t_e)
            i, ps, free = pair()
            v = ps.rearrange("p (h n) -> p h n", h=8)
            i2, ps2, free2 = pair()
            for j in range(8):
                h = hsel(j)
                mm(v[:, h, :], E[:, j, :], vh[:, b, h, :], True, True, *((t_e, t_v) + free if j == 0 else ()))
                t = mm(ps2[:, h:h + 1], E[:, j, :], ones[:, 0:1], True, True, *(free2 if j == 0 else ()), sig=(j == 7))
            copy("dve", hh[:, b], v, t)
            t = copy("dve", sm2[:, 0, b, :], ps2[:, 0:8])
            done(i, t)
            done(i2, t)
            if b == 1:
                i, ps, free = pair()
                i2, ps2, free2 = pair()
                for j in range(8):
                    pa, q = slice(64 * (j // 4), 64 * (j // 4) + 64), j % 4
                    mm(ps[:, 128 * j:128 * j + 128], qs[pa, q, tb], cst[pa, q, 0:128], True, True,
                       *((P.last("dve"),) + free if j == 0 else ()))
                    t = mm(ps2[:, 512 * (j // 4) + q:512 * (j // 4) + q + 1], qs[pa, q, tb], cst[pa, q, 128:129],
                           True, True, *(free2 if j == 0 else ()), sig=(j == 7))
                for j in range(8):
                    h = hsel(j)
                    stt(hh[:, 1, h, :], ps[:, 128 * j:128 * j + 128], colz[:, 1, 2, h:h + 1], hh[:, 1, h, :],
                        ALU.mult, ALU.add, t)
                    o = 512 * (j // 4) + j % 4
                    t1 = stt(sm2[:, 0, 1, h:h + 1], ps2[:, o:o + 1], colz[:, 1, 2, h:h + 1],
                             sm2[:, 0, 1, h:h + 1], ALU.mult, ALU.add)
                done(i, t1)
                done(i2, t1)
            stt(sm2[:, 1, b, :], sm2[:, 0, b, :], -1.0, sm2[:, 0, b, :], ALU.mult, ALU.max)
            tt(sm2[:, 1, b, :], sm2[:, 1, b, :], colz[:, b, 1, :], ALU.max)
            rcp(sm2[:, 2, b, :], sm2[:, 1, b, :])
            tt(hh[:, b], hh[:, b], sm2[:, 2, b, :].unsqueeze(2).broadcast_to([128, 8, 128]), ALU.mult)
            if b == 0:
                i, ps, free = pair()
                for q in range(4):
                    t = tr(ps[:, 128 * q:128 * q + 128], qs[:, 4 + q, 0:128], *((P.last("dve"),) + free if q == 0 else ()),
                           sig=(q == 3))
                gz = colz[:, 0, 2, :].unsqueeze(2).broadcast_to([128, 8, 64])
                t_kg = tt(kg.rearrange("p (h n) -> p h n", n=64), ps[:, 0:512].rearrange("p (h n) -> p h n", n=64),
                          gz, ALU.mult, t)
                done(i, t_kg)
                i, ps, free = pair()
                i2, ps2, free2 = pair()
                for j in range(8):
                    h = hsel(j)
                    pa, q = slice(64 * (j // 4), 64 * (j // 4) + 64), j % 4
                    mm(ps[pa, 512 * (j // 4) + 128 * q:512 * (j // 4) + 128 * q + 128], kg[:, 64 * h:64 * h + 64],
                       vh[:, 0, h, :], True, True, *((t_kg,) + free if j == 0 else ()))
                    t = mm(ps2[pa, 512 * (j // 4) + q:512 * (j // 4) + q + 1], kg[:, 64 * h:64 * h + 64], ones[:, 0:1],
                           True, True, *(free2 if j == 0 else ()), sig=(j == 7))
                for a_ in range(2):
                    pa = slice(64 * a_, 64 * a_ + 64)
                    copy("dve", cst[pa, :, 0:128], ps[pa, 512 * a_:512 * a_ + 512].rearrange("p (q n) -> p q n", q=4), t)
                    t1 = copy("dve", cst[pa, :, 128:129], ps2[pa, 512 * a_:512 * a_ + 4].unsqueeze(2))
                done(i, t1)
                done(i2, t1)
        head_norm(hm, tmp, sm2[:, 4:8], 8, 128, 1e-6)
        tt(hm, hm, mhw.unsqueeze(1).broadcast_to([128, 2, 1024]), ALU.mult)
        t_ym = tt(hm, hm, om, ALU.mult, t_o)
        ymT = qk
        t_ymT = to_fm(hm, ymT, 1024, t_ym)
        mark_mix = top[0]
        P.barrier()
        top[0] = mark_mix
        o0 = mark0 + 2048 + 2048
        mix = big[:, o0:o0 + 4096].rearrange("p (b c) -> p b c", b=2)
        gs = [big[:, o0 + 4096 + 1024 * k:o0 + 5120 + 1024 * k].rearrange("p (b c) -> p b c", b=2) for k in range(2)]
        for c in range(4):
            cs = slice(512 * c, 512 * c + 512)
            for k, (goff, yT, wb) in enumerate(((6448, yrT, "w_br"), (8496, ymT, "w_bm"))):
                proj_a(xT, 16, W, goff + 512 * c, 512,
                       lambda ci, n, v, t, k=k: (actf(gs[k], v, ACT.Sigmoid, t, P.last("dve")),), t_p,
                       bias=bgr[:, 2048 * k + 512 * c:2048 * k + 512 * c + 512])
                tg = P.last("act")

                def eat(ci, n, v, t, k=k, cs=cs, tg=tg):
                    if k == 0:
                        return (tt(mix[:, :, cs], gs[0], v, ALU.mult, t, tg),)
                    t = tt(gs[1], gs[1], v, ALU.mult, t, tg)
                    tt(mix[:, :, cs], mix[:, :, cs], gs[1], ALU.add)
                    return (t,)

                proj_a(yT, 8, I[wb][0], 512 * c, 512, eat)
        P.barrier()
        t_x = P.loads([(x, I["x"][0].rearrange("(b p) d -> p b d", p=128))])
        mixT = xT
        t_mixT = to_fm(mix, mixT, 2048)
        res = x

        def eat_out(res, alpha):
            def f(ci, n, v, t):
                cs = slice(512 * ci, 512 * ci + n)
                return (stt(res[:, :, cs], res[:, :, cs], alpha, v, ALU.mult, ALU.add, t),)
            return f

        P.pending["dve"] = P.pending["dve"] + [t_x]
        proj_a(mixT, 16, I["w_out"][0], 0, 2048, eat_out(res, ALPHA), *t_mixT)

        def layer_norm(v, wn, bn, wt, bt, st, *after):
            t_w = P.loads([(wt, I[wn][0].partition_broadcast(128)), (bt, I[bn][0].partition_broadcast(128))], *after)
            for b in range(2):
                s6 = st[:, 24 * b:24 * b + 24]
                for c in range(4):
                    P.dve(lambda g, b=b, c=c, s6=s6: g.bn_stats(s6[:, 6 * c:6 * c + 6], v[:, b, 512 * c:512 * c + 512]))
                P.dve(lambda g, b=b, s6=s6: g.bn_aggr(st[:, 48 + 2 * b:50 + 2 * b], s6))
                t = ts(st[:, 52 + b:53 + b], st[:, 49 + 2 * b:50 + 2 * b], 1e-5, None, ALU.add)
                t = actf(st[:, 54 + b:55 + b], st[:, 52 + b:53 + b], ACT.Sqrt, t)
                rcp(st[:, 56 + b:57 + b], st[:, 54 + b:55 + b], t)
                ts(v[:, b, :], v[:, b, :], st[:, 48 + 2 * b:49 + 2 * b], st[:, 56 + b:57 + b], ALU.subtract, ALU.mult)
                tt(v[:, b, :], v[:, b, :], wt, ALU.mult, t_w)
                t = tt(v[:, b, :], v[:, b, :], bt, ALU.add)
            return t

        P.barrier()
        top[0] = mark_x + 4096
        wt, bt, st = alloc(2048), alloc(2048), alloc(64)
        t_x1 = layer_norm(x, "ln1_w", "ln1_b", wt, bt, st)
        x1T = xT
        t_x1T = to_fm(x, x1T, 2048, t_x1)
        P.barrier()
        top[0] = mark_x + 4096

        wr = alloc(16 * 36).rearrange("p (k n) -> p k n", k=16)
        br = alloc(36)
        wg = alloc(64).rearrange("p (b e) -> p b e", b=2)
        rs = alloc(2 * 160).rearrange("p (b n) -> p b n", b=2)
        t_r = P.loads([(wr[:, :, 0:4], I["w_rg"][0].rearrange("(k p) n -> p k n", p=128)),
                       (wr[:, :, 4:36], I["w_re"][0].rearrange("(k p) n -> p k n", p=128)),
                       (br[0:1, 0:4], I["b_rg"]), (br[0:1, 4:36], I["b_re"])])
        i, ps, free = pair()
        for b in range(2):
            o = ps[:, 512 * b:512 * b + 36]
            mm(o, ones[0:1, 0:128], br[0:1, :], True, False, t_r, *(free if b == 0 else ()))
            for k in range(16):
                t = mm(o, x1T[:, k, 128 * b:128 * b + 128], wr[:, k, :], False, k == 15, sig=(k == 15))
        for b in range(2):
            s = rs[:, b, :]
            lg, le0 = s[:, 0:4], s[:, 4:36]
            copy("dve", s[:, 0:36], ps[:, 512 * b:512 * b + 36], t)
            if b == 1:
                done(i, P.last("dve"))

            def first_max(l, n, m, o, s1):
                red(m, l, ALU.max)
                ts(s1[:, 1:1 + n], l, m, None, ALU.is_ge)
                mset(s1[:, 0:1], 0.0)
                scan(s1[:, 1:1 + n], s1[:, 1:1 + n], s1[:, 1:1 + n], 0.0, ALU.max, ALU.max)
                return tt(o, s1[:, 1:1 + n], s1[:, 0:n], ALU.subtract)

            gm, og, nm, ex, gw = s[:, 36:37], s[:, 37:41], s[:, 41:42], s[:, 42:46], s[:, 46:47]
            scr = s[:, 48:60]
            first_max(lg, 4, gm, og, scr)
            t1 = ts(nm, gm, -1.0, None, ALU.mult)
            t1 = actf(ex, lg, ACT.Exp, t1, bias=nm)
            red(gw, ex, ALU.add, t1)
            rcp(gw, gw)
            le, o1, le2, o2 = s[:, 60:68], s[:, 68:76], s[:, 76:84], s[:, 84:92]
            m1, m2, w1, w2 = s[:, 92:93], s[:, 93:94], s[:, 94:95], s[:, 95:96]
            ts(le, le0[:, 0:8], og[:, 0:1], None, ALU.mult)
            for g_ in range(1, 4):
                stt(le, le0[:, 8 * g_:8 * g_ + 8], og[:, g_:g_ + 1], le, ALU.mult, ALU.add)
            first_max(le, 8, m1, o1, scr)
            stt(le2, o1, NEG, le, ALU.mult, ALU.add)
            first_max(le2, 8, m2, o2, scr)
            t1 = tt(w2, m2, m1, ALU.subtract)
            t1 = actf(w2, w2, ACT.Exp, t1)
            ts(w1, w2, 1.0, None, ALU.add, None, t1)
            rcp(w1, w1)
            tt(w1, w1, gw, ALU.mult)
            tt(w2, w2, w1, ALU.mult)
            ts(o1, o1, w1, None, ALU.mult)
            stt(o1, o2, w2, o1, ALU.mult, ALU.add)
            for g_ in range(4):
                t_wg = ts(wg[:, b, 8 * g_:8 * g_ + 8], o1, og[:, g_:g_ + 1], None, ALU.mult)

        acc = x
        t_acc = ts(acc, acc, ALPHA, None, ALU.mult)
        sg = [tm(512) for _ in range(2)]
        hb = [tm(512) for _ in range(2)]
        hT = [fm(4) for _ in range(2)]
        t_hT = [(), ()]
        pend = None

        def down(e, z, toks):
            for c in range(4):
                cs = slice(512 * c, 512 * c + 512)

                def eat(ci, n, v, t, cs=cs, e=e):
                    for b in range(2):
                        t1 = stt(acc[:, b, cs], v[:, b, :], wg[:, b, e:e + 1], acc[:, b, cs], ALU.mult, ALU.add, t)
                    return (t1,)

                proj_a(hT[z], 4, I["w_down"][0, e], 512 * c, 512, eat, *toks)

        for e in range(32):
            z = e % 2
            tk = {}
            proj_a(x1T, 16, I["w_gate"][0, e], 0, 512,
                   lambda ci, n, v, t, z=z: (actf(sg[z], v, ACT.Sigmoid, t, P.last("dve")),
                                             tt(sg[z], sg[z], v, ALU.mult, P.last("act"))))
            proj_a(x1T, 16, I["w_up"][0, e], 0, 512,
                   lambda ci, n, v, t, z=z: (tt(hb[z], sg[z], v, ALU.mult, t),))
            if pend is not None:
                down(*pend)
            tk = to_fm(hb[z], hT[z], 512, P.last("dve"))
            pend = (e, z, tk)
        down(*pend)

        P.barrier()
        top[0] = mark_x + 4096
        pt = tm(256)
        pT = fm(2)
        gs = tm(512)
        t_pl = P.loads([(pt, I["p"][0, 0].rearrange("(b p) d -> p b d", p=128))])
        i, ps, free = pair()
        v = ps.rearrange("p (k b t) -> p k b t", k=4, b=2)
        for b in range(2):
            for k in range(2):
                t = tr(v[:, k, b, :], pt[:, b, 128 * k:128 * k + 128], *((t_pl,) + free if b + k == 0 else ()),
                       sig=(b + k == 2))
        t_pT = copy("dve", pT.rearrange("p k (b t) -> p k b t", b=2), v[:, 0:2], t)
        done(i, t_pT)
        for c in range(4):
            cs = slice(512 * c, 512 * c + 512)
            proj_a(x1T, 16, I["w_pg"][0], 512 * c, 512,
                   lambda ci, n, v, t: (actf(gs, v, ACT.Sigmoid, t, P.last("dve")),))

            def eat(ci, n, v, t, cs=cs):
                t = tt(gs, gs, v, ALU.mult, t, P.last("act"))
                tt(acc[:, :, cs], acc[:, :, cs], gs, ALU.add)
                return (t,)

            proj_a(pT, 2, I["w_ple"][0], 512 * c, 512, eat, t_pT)
        P.barrier()
        top[0] = mark_x + 4096
        wt, bt, st = alloc(2048), alloc(2048), alloc(64)
        t_x2 = layer_norm(x, "ln2_w", "ln2_b", wt, bt, st)

        def rms(v, gsrc, o, wt, st, *after):
            t_w = P.loads([(wt, gsrc.partition_broadcast(128))], *after)
            for b in range(2):
                tt(o[:, b, :], v[:, b, :], v[:, b, :], ALU.mult)
                red(st[:, b:b + 1], o[:, b, :], ALU.add)
                t = ts(st[:, 2 + b:3 + b], st[:, b:b + 1], 1.0 / 2048, 1e-6, ALU.mult, ALU.add)
                t = actf(st[:, 4 + b:5 + b], st[:, 2 + b:3 + b], ACT.Sqrt, t)
                rcp(st[:, 6 + b:7 + b], st[:, 4 + b:5 + b], t)
                t = stt(o[:, b, :], v[:, b, :], st[:, 6 + b:7 + b], wt, ALU.mult, ALU.mult, t_w)
            return t

        P.barrier()
        top[0] = mark_x + 4096
        markh = top[0]
        hT_ = xT
        hn = tm(2048)
        wt, st = alloc(2048), alloc(64)
        t_h = rms(x, I["norm_even_g_2"][0], hn, wt, st)
        t_hT_ = to_fm(hn, hT_, 2048, t_h)
        P.barrier()
        top[0] = markh
        We = I["w_in_even_2"][0]
        oT = fm(16)
        uT, zb = fm(8), fm(8)
        mark_s5 = top[0]
        qT, kT, za = fm(8), fm(8), fm(8)
        vv = tm(1024)
        bw = alloc(4096).rearrange("p (h x) -> p h x", h=16)
        sc = alloc(1536)
        pr = alloc(1536).rearrange("p (j t) -> p j t", j=12)
        mx = alloc(64).rearrange("p (k b h) -> p k b h", k=8, b=2)
        t_bw = P.loads([(bw, I["bias_windows"])])
        proj_b(hT_, 16, We, 0, 1024, lambda ci, v, t: (copy("act", qT[:, 4 * ci:4 * ci + 4, :], v, t, scale=0.125),),
               *t_hT_)
        proj_b(hT_, 16, We, 1024, 1024, lambda ci, v, t: (copy("act", kT[:, 4 * ci:4 * ci + 4, :], v, t),))
        proj_a(hT_, 16, We, 2048, 1024, lambda ci, n, v, t: (copy("act", vv[:, :, 512 * ci:512 * ci + n], v, t),))
        proj_b(hT_, 16, We, 3072, 1024, lambda ci, v, t: (copy("act", uT[:, 4 * ci:4 * ci + 4, :], v, t),))

        def silu_into(dst):
            def f(ci, v, t):
                d = dst[:, 4 * ci:4 * ci + 4, :]
                t1 = actf(d, v, ACT.Sigmoid, t)
                return (tt(d, d, v, ALU.mult, t1),)
            return f

        proj_b(hT_, 16, We, 4096, 1024, silu_into(za))
        proj_b(hT_, 16, We, 5120, 1024, silu_into(zb))
        t_qkv = P.last("act")
        t_za = P.last("dve")

        def softmax_turn(h4, after):
            s4 = sc.rearrange("p (h x) -> p h x", h=4)
            parts = (s4[:, :, 0:128], s4[:, :, 128:384])
            for b in range(2):
                n = 128 * (b + 1)
                red(mx[:, 0, b, :], parts[b], ALU.max, *after)
                tt(parts[b], parts[b], mx[:, 0, b, :].unsqueeze(2).broadcast_to([128, 4, n]), ALU.subtract)
            t = actf(sc, sc, ACT.Exp, P.last("dve"))
            for b in range(2):
                n = 128 * (b + 1)
                red(mx[:, 1, b, :], parts[b], ALU.add, t)
                rcp(mx[:, 2, b, :], mx[:, 1, b, :])
                t1 = tt(parts[b], parts[b], mx[:, 2, b, :].unsqueeze(2).broadcast_to([128, 4, n]), ALU.mult)
            toks = []
            for half in range(2):
                i, ps, free = pair()
                for j in range(6):
                    m = 6 * half + j
                    off = 512 * (j // 3) + 128 * (j % 3)
                    t = tr(ps[:, off:off + 128], sc[:, 128 * m:128 * m + 128], *((t1,) + free if j == 0 else ()),
                           sig=(j == 5))
                t = copy("act", pr[:, 6 * half:6 * half + 6, :].rearrange("p (a k) t -> p a k t", a=2),
                         ps.rearrange("p (a x) -> p a x", a=2)[:, :, 0:384].rearrange("p a (k t) -> p a k t", k=3),
                         t, P.last("pe"))
                done(i, t)
            return t

        for u in range(4):
            i, ps, free = pair()
            i2, ps2, free2 = pair()
            pp = (ps, ps2)
            for j in range(4):
                h = 4 * u + j
                pa, q = slice(64 * (h % 2), 64 * (h % 2) + 64), h // 2
                o = pp[j % 2][:, 512 * (j // 2):512 * (j // 2) + 384]
                mm(o[:, 0:128], qT[pa, q, 0:128], kT[pa, q, 0:128], True, True,
                   *(free + (t_qkv,) if j == 0 else free2 if j == 1 else ()))
                t = mm(o[:, 128:384], qT[pa, q, 128:256], kT[pa, q, 0:256], True, True, sig=(j == 3))
            s4 = sc.rearrange("p (h x) -> p h x", h=4)
            for j in range(4):
                o = pp[j % 2][:, 512 * (j // 2):512 * (j // 2) + 384]
                bwh = bw[:, 4 * u + j, :]
                tt(s4[:, j, 0:128], o[:, 0:128], bwh[:, 128:256], ALU.add, t, t_bw, P.last("pe"))
                t1 = tt(s4[:, j, 128:384], o[:, 128:384], bwh, ALU.add)
            done(i, t1)
            done(i2, t1)
            mset(s4[0:64, :, 64:128], NEG)
            mset(s4[0:64, :, 320:384], NEG)
            t_pr = softmax_turn(4, ())
            i, ps, free = pair()
            for j in range(4):
                h = 4 * u + j
                o = ps[64 * (j % 2):64 * (j % 2) + 64, 512 * (j // 2):512 * (j // 2) + 256]
                mm(o, vv[:, 0, 64 * h:64 * h + 64], pr[:, 3 * j:3 * j + 2, :].rearrange("p a t -> p (a t)"), True, False,
                   *(free + (t_pr,) if j == 0 else ()))
                t = mm(o[:, 128:256], vv[:, 1, 64 * h:64 * h + 64], pr[:, 3 * j + 2, :], False, True, sig=(j == 3))
            t = tt(oT[:, 2 * u:2 * u + 2, :], ps.rearrange("p (a x) -> p a x", a=2)[:, :, 0:256],
                   za[:, 2 * u:2 * u + 2, :], ALU.mult, t, t_za)
            done(i, t)

        P.barrier()
        top[0] = mark_s5
        lr, li, ld = alloc(32), alloc(32), alloc(32)
        bre, bim, cre, cim = [alloc(512).rearrange("p (i c) -> p i c", i=32) for _ in range(4)]
        dsk, bgl = alloc(8), alloc(8)
        V = [alloc(32) for _ in range(14)]
        Bb = [alloc(512).rearrange("p (i c) -> p i c", i=32) for _ in range(3)]
        pads = [alloc(640) for _ in range(4)]
        BT = [alloc(512).rearrange("p (i c) -> p i c", i=4) for _ in range(2)]
        CC, SS = [alloc(1024).rearrange("p (i t) -> p i t", i=4) for _ in range(2)]
        M1, M2, Z1, Z2 = [alloc(1024).rearrange("p (i t) -> p i t", i=4) for _ in range(4)]
        yT = fm(8)
        t_s = P.loads([(lr, I["s5_lr"]), (li, I["s5_li"]),
                       (ld[0:64, :], I["s5_ld"][0].partition_broadcast(64)),
                       (ld[64:128, :], I["s5_ld"][1].partition_broadcast(64)),
                       (bre, I["s5_bre"]), (bim, I["s5_bim"]), (cre, I["s5_cre"]), (cim, I["s5_cim"]),
                       (dsk, I["s5_dd"]), (bgl, I["bglu"])])
        dt, mag, ang, k2, sn, cs_, are, aim, den, cr, ci_, tA, tB, tC = V
        actf(dt, ld, ACT.Exp, t_s)
        t = tt(mag, lr, dt, ALU.mult, P.last("act"))
        t = actf(mag, mag, ACT.Exp, t)
        tt(ang, li, dt, ALU.mult, t)
        TP = 2 * math.pi
        C1 = 6.28125
        C2 = 2029.0 / 2 ** 20
        C3 = TP - C1 - C2
        MG = 12582912.0
        ts(k2, ang, 1.0 / TP, MG, ALU.mult, ALU.add)
        ts(k2, k2, -MG, None, ALU.add)
        stt(ang, k2, -C1, ang, ALU.mult, ALU.add)
        stt(ang, k2, -C2, ang, ALU.mult, ALU.add)
        stt(ang, k2, -C3, ang, ALU.mult, ALU.add)
        PI = 3.1415925
        ts(sn, ang, PI, -PI, ALU.min, ALU.max)
        ts(cs_, ang, math.pi / 2, None, ALU.add)
        ts(tA, cs_, PI, -TP, ALU.is_gt, ALU.mult)
        tt(cs_, cs_, tA, ALU.add)
        ts(cs_, cs_, PI, -PI, ALU.min, ALU.max)
        actf(sn, sn, ACT.Sin, P.last("dve"))
        t = actf(cs_, cs_, ACT.Sin)
        tt(are, mag, cs_, ALU.mult, t)
        tt(aim, mag, sn, ALU.mult)
        tt(tA, lr, lr, ALU.mult)
        tt(tB, li, li, ALU.mult)
        tt(den, tA, tB, ALU.add)
        rcp(den, den)
        ts(are, are, -1.0, None, ALU.add)
        tt(tA, are, lr, ALU.mult)
        tt(tB, aim, li, ALU.mult)
        tt(tA, tA, tB, ALU.add)
        tt(cr, tA, den, ALU.mult)
        tt(tA, aim, lr, ALU.mult)
        tt(tB, are, li, ALU.mult)
        tt(tA, tA, tB, ALU.subtract)
        tt(ci_, tA, den, ALU.mult)
        crb = cr.unsqueeze(2).broadcast_to([128, 32, 16])
        cib = ci_.unsqueeze(2).broadcast_to([128, 32, 16])
        tt(Bb[0], bre, crb, ALU.mult)
        tt(Bb[2], bim, cib, ALU.mult)
        tt(Bb[0], Bb[0], Bb[2], ALU.subtract)
        tt(Bb[1], bim, crb, ALU.mult)
        tt(Bb[2], bre, cib, ALU.mult)
        tt(Bb[1], Bb[1], Bb[2], ALU.add)
        ts(cim, cim, -1.0, None, ALU.mult)
        for z in pads:
            mset(z, 0.0)
        for j in range(8):
            for z, src in zip(pads, (Bb[0], Bb[1], cre, cim)):
                d = z.rearrange("p (i x) -> p i x", i=4)
                for hf in range(2):
                    pa = slice(64 * hf, 64 * hf + 64)
                    t_pd = P.dve(lambda g, d=d, src=src, pa=pa, hf=hf, j=j: g.tensor_copy(
                        d[pa, :, 16 * hf:16 * hf + 16], src[pa, 4 * j:4 * j + 4, :]), P.last("pe"))
            for z in range(2):
                i, ps, free = pair()
                for q in range(4):
                    t = tr(ps[:, 128 * q:128 * q + 128], pads[z][:, 128 * q:128 * q + 128],
                           *((t_pd,) + free if q == 0 else ()), sig=(q == 3))
                t_bt = copy("dve", BT[z], ps[:, 0:512].rearrange("p (i c) -> p i c", i=4), t)
                done(i, t_bt)
            j4 = slice(4 * j, 4 * j + 4)
            mset(CC[:, :, 0:1], 1.0)
            mset(SS[:, :, 0:1], 0.0)
            copy("dve", CC[:, :, 1:2], cs_[:, j4].unsqueeze(2))
            copy("dve", SS[:, :, 1:2], sn[:, j4].unsqueeze(2))
            for l in range(8):
                n = 1 << l
                w = min(n, 255 - n)
                src = slice(1, 1 + w)
                dst = slice(n + 1, n + 1 + w)
                cb = CC[:, :, n:n + 1].broadcast_to([128, 4, w])
                sb_ = SS[:, :, n:n + 1].broadcast_to([128, 4, w])
                tt(M1[:, :, 0:w], CC[:, :, src], cb, ALU.mult)
                tt(M2[:, :, 0:w], SS[:, :, src], sb_, ALU.mult)
                tt(Z1[:, :, 0:w], CC[:, :, src], sb_, ALU.mult)
                tt(Z2[:, :, 0:w], SS[:, :, src], cb, ALU.mult)
                tt(CC[:, :, dst], M1[:, :, 0:w], M2[:, :, 0:w], ALU.subtract)
                tt(SS[:, :, dst], Z1[:, :, 0:w], Z2[:, :, 0:w], ALU.add)
            i, ps, free = pair()
            i2, ps2, free2 = pair()
            br_, bi_ = [z.rearrange("p (i t) -> p i t", i=4) for z in (ps, ps2)]
            for q in range(4):
                mm(br_[:, q, :], BT[0][:, q, :], uT[:, j, :], True, True, *((t_bt,) + free if q == 0 else ()))
                t = mm(bi_[:, q, :], BT[1][:, q, :], uT[:, j, :], True, True, *(free2 if q == 0 else ()), sig=(q == 3))
            tt(M1, br_, CC, ALU.mult, t)
            tt(M2, bi_, SS, ALU.mult)
            tt(M1, M1, M2, ALU.add)
            tt(M2, bi_, CC, ALU.mult)
            t = tt(Z1, br_, SS, ALU.mult)
            done(i, t)
            done(i2, t)
            tt(M2, M2, Z1, ALU.subtract)
            for q in range(4):
                mg = mag[:, 4 * j + q:4 * j + q + 1].broadcast_to([128, 256])
                scan(Z1[:, q, :], mg, M1[:, q, :], 0.0, ALU.mult, ALU.add)
                scan(Z2[:, q, :], mg, M2[:, q, :], 0.0, ALU.mult, ALU.add)
            tt(M1, Z1, CC, ALU.mult)
            tt(M2, Z2, SS, ALU.mult)
            tt(M1, M1, M2, ALU.subtract)
            tt(M2, Z1, SS, ALU.mult)
            tt(Z2, Z2, CC, ALU.mult)
            t = tt(M2, M2, Z2, ALU.add)
            i, ps, free = pair()
            for q in range(4):
                mm(ps[:, 0:256], pads[2][:, 128 * q:128 * q + 128], M1[:, q, :], q == 0, False,
                   *((t,) + free if q == 0 else ()))
                t1 = mm(ps[:, 0:256], pads[3][:, 128 * q:128 * q + 128], M2[:, q, :], False, q == 3, sig=(q == 3))
            y1 = yT[:, j, :]
            t = stt(y1, uT[:, j, :], dsk[:, j:j + 1], ps[:, 0:256], ALU.mult, ALU.add, t1)
            done(i, t)
            tt(Z1[:, 0, :], y1, y1, ALU.mult)
            ts(Z1[:, 0, :], Z1[:, 0, :], 0.044715, 1.0, ALU.mult, ALU.add)
            t = tt(Z1[:, 0, :], Z1[:, 0, :], y1, ALU.mult)
            t = actf(Z1[:, 0, :], Z1[:, 0, :], ACT.Tanh, t, scale=math.sqrt(2 / math.pi))
            ts(y1, y1, 0.5, None, ALU.mult)
            t_yT = stt(y1, Z1[:, 0, :], 1.0, y1, ALU.add, ALU.mult, t)

        gt = M1

        def eat_glu(ci, v, t):
            for m in range(4):
                t1 = actf(gt[:, m, :], v[:, m, :], ACT.Sigmoid, t, P.last("dve"), bias=bgl[:, 4 * ci + m:4 * ci + m + 1])
            tt(gt, gt, yT[:, 4 * ci:4 * ci + 4, :], ALU.mult, t1)
            tt(oT[:, 8 + 4 * ci:12 + 4 * ci, :], gt, zb[:, 4 * ci:4 * ci + 4, :], ALU.mult)
            return (t1,)

        proj_b(yT, 8, I["w_glu_2"][0], 0, 1024, eat_glu, t_yT)
        proj_a(oT, 16, I["w_out_even_2"][0], 0, 2048, eat_out(x, 1.0), P.last("dve"))

        P.barrier()
        top[0] = markh
        hn = tm(2048)
        wt, st = alloc(2048), alloc(64)
        t_h = rms(x, I["norm_odd_g_2"][0], hn, wt, st)
        t_hT_ = to_fm(hn, hT_, 2048, t_h)
        P.barrier()
        top[0] = markh
        Wo = I["w_in_odd_2"][0]
        qT, kT, zT, oT = fm(16), fm(16), fm(16), fm(16)
        vv = tm(2048)
        fr = alloc(1024).rearrange("p (k t) -> p k t", t=256)
        bf = cols[:, 3:4]
        sc = alloc(1536)
        pr = alloc(1536).rearrange("p (j t) -> p j t", j=12)
        mx = alloc(64).rearrange("p (k b h) -> p k b h", k=8, b=2)
        t_bf = P.loads([(bf[0:16, 0:1], I["b_forget_2"].rearrange("o h -> h o"))])
        i, ps, free = pair()
        for g0 in range(0, 16, 4):
            s, sl, tok = piece(Wo[128 * g0:128 * g0 + 512, 8192:8208].rearrange("(k p) n -> p k n", p=128), 4, 16)
            for k in range(4):
                t = mm(ps[0:16, 0:256], sl[:, k, :], hT_[:, g0 + k, :], g0 + k == 0, g0 + k == 15, tok,
                       *(free + t_hT_ if g0 + k == 0 else ()), sig=(k == 3))
            P.slot_free[s] = t
        F = [fr[0:16, k, :] for k in range(4)]
        t = ts(F[0], ps[0:16, 0:256], bf[0:16, 0:1], None, ALU.add, None, t, t_bf)
        done(i, t)
        log_sigmoid(F[0], F[1], F[2])
        mset(F[1], 1.0)
        scan(F[3], F[1], F[2], 0.0, ALU.mult, ALU.subtract)
        t_f = P.last("dve")
        proj_b(hT_, 16, Wo, 0, 2048, lambda ci, v, t: (
            copy("act", qT[:, 4 * ci:4 * ci + 4, :], v, t, scale=1.0 / math.sqrt(128.0)),))
        proj_b(hT_, 16, Wo, 2048, 2048, lambda ci, v, t: (copy("act", kT[:, 4 * ci:4 * ci + 4, :], v, t),))
        proj_a(hT_, 16, Wo, 4096, 2048, lambda ci, n, v, t: (copy("act", vv[:, :, 512 * ci:512 * ci + n], v, t),))
        proj_b(hT_, 16, Wo, 6144, 2048, silu_into(zT))
        t_qkv = P.last("act")
        t_za = P.last("dve")
        for u in range(4):
            s4 = sc.rearrange("p (h x) -> p h x", h=4)
            for g2 in range(2):
                i, ps, free = pair()
                for j in range(2):
                    h = 4 * u + 2 * g2 + j
                    o = ps[:, 512 * j:512 * j + 384]
                    mm(o[:, 0:128], qT[:, h, 0:128], kT[:, h, 0:128], True, False,
                       *(free + (t_qkv, t_f) if j == 0 else ()))
                    mm(o[:, 0:128], sel[0:16, h, :], F[3][:, 0:128], False, True)
                    mm(o[:, 128:384], qT[:, h, 128:256], kT[:, h, :], True, False)
                    t = mm(o[:, 128:384], sel[0:16, h, :], F[3], False, True, sig=(j == 1))
                cmb = cmask.unsqueeze(1).broadcast_to([128, 2, 128])
                po = ps.rearrange("p (a x) -> p a x", a=2)
                so = s4[:, 2 * g2:2 * g2 + 2, :]
                tt(so[:, :, 0:128], po[:, :, 0:128], cmb, ALU.add, t, P.last("pe"))
                copy("dve", so[:, :, 128:256], po[:, :, 128:256])
                t1 = tt(so[:, :, 256:384], po[:, :, 256:384], cmb, ALU.add)
                done(i, t1)
            t_pr = softmax_turn(4, ())
            for g2 in range(2):
                i, ps, free = pair()
                for j in range(2):
                    m = 2 * g2 + j
                    h = 4 * u + m
                    o = ps[:, 512 * j:512 * j + 256]
                    mm(o, vv[:, 0, 128 * h:128 * h + 128], pr[:, 3 * m:3 * m + 2, :].rearrange("p a t -> p (a t)"),
                       True, False, *(free + (t_pr,) if j == 0 else ()))
                    t = mm(o[:, 128:256], vv[:, 1, 128 * h:128 * h + 128], pr[:, 3 * m + 2, :], False, True,
                           sig=(j == 1))
                hs = slice(4 * u + 2 * g2, 4 * u + 2 * g2 + 2)
                t = tt(oT[:, hs, :], ps.rearrange("p (a x) -> p a x", a=2)[:, :, 0:256], zT[:, hs, :], ALU.mult, t, t_za)
                done(i, t)
        proj_a(oT, 16, I["w_out_odd_2"][0], 0, 2048, eat_out(x, 1.0), P.last("dve"))
        P.barrier()
        top[0] = markh
        hn = tm(2048)
        wt, st = alloc(2048), alloc(64)
        t_h = rms(x, I["final_norm_g_2"], hn, wt, st)
        dump(hn, t_h)


_PLAIN = ["x", "p", "w_in", "mu_shift", "w0", "w_w2", "a0", "w_a2", "w_g2", "k_k", "k_a", "r_k", "lnx_w", "lnx_b",
          "i_bias", "f_bias", "mh_w", "b_gate", "w_br", "w_bm", "w_out", "ln1_w", "ln1_b", "w_rg", "b_rg", "w_re",
          "b_re", "w_gate", "w_up", "w_down", "w_pg", "w_ple", "ln2_w", "ln2_b", "norm_even_g_2", "w_in_even_2",
          "w_glu_2", "w_out_even_2", "norm_odd_g_2", "w_in_odd_2", "b_forget_2", "w_out_odd_2", "final_norm_g_2"]


def kernel(**inputs):
    import numpy as np
    import concourse.bacc as _bacc
    from concourse import mybir as _mybir
    from concourse.bass_utils import run_bass_kernel_spmd as _run

    a = {k: np.ascontiguousarray(inputs[k]) for k in _PLAIN}
    conv = np.concatenate([np.asarray(inputs["conv_w"])[0], np.asarray(inputs["conv_b"])], 0)
    a["conv"] = np.ascontiguousarray(conv.reshape(5, 8, 128).transpose(2, 0, 1))
    rel = np.asarray(inputs["rel_bias_2"])[0]
    idx = np.clip(np.arange(128)[:, None] - np.arange(256)[None, :] + 128, -128, 128) + 128
    a["bias_windows"] = np.ascontiguousarray(rel[:, idx].transpose(1, 0, 2))
    pk = lambda n: np.ascontiguousarray(np.asarray(inputs[n])[0].reshape(32, 128).T)
    a["s5_lr"], a["s5_li"] = pk("s5_lambda_re_2"), pk("s5_lambda_im_2")
    a["s5_ld"] = np.ascontiguousarray(np.asarray(inputs["s5_log_dt_2"])[0].reshape(32, 2).T)
    for k, n in (("s5_bre", "s5_b_re_2"), ("s5_bim", "s5_b_im_2")):
        a[k] = np.ascontiguousarray(np.asarray(inputs[n])[0].reshape(32, 128, 16).transpose(1, 0, 2))
    for k, n in (("s5_cre", "s5_c_re_2"), ("s5_cim", "s5_c_im_2")):
        a[k] = np.ascontiguousarray(
            np.asarray(inputs[n])[0].reshape(32, 2, 16, 64).transpose(1, 3, 0, 2).reshape(128, 32, 16))
    a["s5_dd"] = np.ascontiguousarray(np.asarray(inputs["s5_d_2"])[0].reshape(8, 128).T)
    a["bglu"] = np.ascontiguousarray(np.asarray(inputs["b_glu_2"])[0].reshape(8, 128).T)

    nc = _bacc.Bacc("TRN2", target_bir_lowering=False, num_devices=1)
    arrays, args = {}, {}
    for k, v in a.items():
        arrays["in_" + k] = v
        args[k] = nc.dram_tensor("in_" + k, v.shape, _mybir.dt.from_np(v.dtype), kind="ExternalInput").ap()
    out = nc.dram_tensor("out_0", (1, 256, 2048), _mybir.dt.float32, kind="ExternalOutput").ap()
    build(nc, args, out)
    r = _run(nc, [arrays], core_ids=[0])
    return r.results[0]["out_0"]
```

```python
import math

import concourse.bass as bass
from concourse import mybir

F32 = mybir.dt.float32
F32R = mybir.dt.float32r
ALU = mybir.AluOpType
ACT = mybir.ActivationFunctionType
AX = mybir.AxisListType
CAP = 64
LORA = ("w_w2", "w_a2", "w_g2")
ALPHA = 2.0 ** 0.25
NEG = -1e30


class Prog:

    def __init__(self, nc, ctx, name, bufs, ahead, look):
        self.nc = nc
        self.ctx = ctx
        self.q = {e: [] for e in ("pe", "dve", "act", "pool", "sp")}
        self.n = {e: 0 for e in self.q}
        self.name = name
        self.sem = {e: ctx.enter_context(nc.semaphore(f"{name}_{e}")) for e in self.q}
        self.pending = {e: [] for e in self.q}
        self.dma_open = []
        self.nb = 0
        self.raw, self.hi, self.lo = bufs
        self.slot_sem = [ctx.enter_context(nc.semaphore(f"{name}_slot{i}")) for i in range(len(self.raw))]
        self.slot_free = [None] * len(self.raw)
        self.half_free = [None] * len(self.hi)
        self.specs = []
        self.ahead = ahead
        self.look = look
        self.issued = []
        self.halves = 0
        self.pair_i = 0
        self.pair_free = [()] * 4
        self.pe_signed = True

    def put(self, e, fn, after, sig):
        waits = [t for t in self.pending[e] + list(after) if t is not None]
        self.pending[e] = []
        if sig:
            self.n[e] += 1
        self.q[e].append((fn, waits, (self.sem[e], 1) if sig else None))
        return (self.sem[e], self.n[e]) if sig else None

    def last(self, e):
        return (self.sem[e], self.n[e])

    def pe(self, fn, *after, sig=False):
        self.pe_signed = sig
        return self.put("pe", fn, after, sig)

    def dve(self, fn, *after):
        return self.put("dve", fn, (self.last("dve"),) + after, True)

    def act(self, fn, *after):
        return self.put("act", fn, (self.last("act"),) + after, True)

    def pool(self, fn, *after):
        return self.put("pool", fn, (self.last("pool"),) + after, True)

    def loads(self, pairs, *after, e="pool"):
        s = self.ctx.enter_context(self.nc.semaphore(f"{self.name}_dma{self.nb}"))
        self.nb += 1
        waits = [t for t in self.pending[e] + list(after) if t is not None]
        self.pending[e] = []
        for i, (out, in_) in enumerate(pairs):
            self.q[e].append((lambda g, out=out, in_=in_: g.dma_start(out, in_), waits if i == 0 else [], (s, 16)))
        t = (s, 16 * len(pairs))
        self.dma_open.append(t)
        return t

    def barrier(self):
        assert self.pe_signed
        toks = [self.last(e) for e in ("pe", "dve", "act", "pool")] + self.dma_open
        self.dma_open = []
        for e in ("pe", "dve", "act", "pool"):
            self.pending[e] = self.pending[e] + toks

    def branch(self, e, eng, seen, waits, flag, rest):
        ready, all_done = waits
        if seen.get(id(ready[0]), (0, 0))[0] < ready[1]:
            eng.wait_ge(*ready)
            seen[id(ready[0])] = (ready[1], 0)
        with eng.If(eng.value_load(flag, min_val=0, max_val=1) > 0):
            for s, v in all_done:
                if v:
                    eng.wait_ge(s, v)
            rest.emit(e, eng)
            for o in ("pe", "dve", "act"):
                eng.wait_ge(*rest.last(o))

    def emit(self, e, eng):
        seen = {}
        for fn, waits, inc in self.q[e]:
            if isinstance(fn, tuple):
                self.branch(e, eng, seen, waits, *fn)
                continue
            need = {}
            for s, v in waits:
                k = id(s)
                if v > seen.get(k, (0, 0))[0] and v > need.get(k, (None, 0))[1]:
                    need[k] = (s, v)
            for k, (s, v) in need.items():
                eng.wait_ge(s, v)
                seen[k] = (v, 0)
            if fn is None:
                continue
            ins = fn(eng)
            if inc:
                ins.then_inc(inc[0], inc[1])


def bcast(ap, shape):
    return ap.broadcast_to(shape)


def build(nc, I, out, plan=None):
    from contextlib import ExitStack

    with ExitStack() as ctx:
        TOT = 53208
        arena = ctx.enter_context(nc.sbuf_tensor("arena", [128, TOT], F32))
        base = nc.sbuf_base - 4 * TOT
        named = [0]
        psum = ctx.enter_context(nc.psum_tensor("psum", [128, 4096], F32))
        top = [0]

        def at(o, n, dt=F32):
            named[0] += 1
            assert o + n <= TOT, o + n
            return nc.alloc_sbuf_tensor_at(f"t{named[0]}", [128, n], dt, offset=base + 4 * o)[:, :]

        def alloc(n, dt=F32):
            o = top[0]
            top[0] = o + n + -n % 8
            return at(o, n, dt)

        def tm(c):
            return alloc(2 * c).rearrange("p (b c) -> p b c", b=2)

        def fm(k):
            return alloc(k * 256).rearrange("p (k t) -> p k t", t=256)

        def alloc_r(n):
            return alloc(n, F32R)

        def alloc_bufs(nraw, nhalf):
            return ([alloc(1024) for _ in range(nraw)], [alloc_r(1024) for _ in range(nhalf)],
                    [alloc_r(1024) for _ in range(nhalf)])

        plans = plan or {}
        P = Prog(nc, ctx, "s", alloc_bufs(6, 3), plans.get("s", []), 2)
        planned = {"s": P.specs}

        def pair():
            i = P.pair_i
            while P.pair_free[i] is None:
                i = (i + 1) % 4
            P.pair_i = (i + 1) % 4
            free = P.pair_free[i]
            P.pair_free[i] = None
            return i, psum[:, 1024 * i:1024 * i + 1024], free

        def done(i, *toks):
            P.pair_free[i] = toks

        def issue(spec):
            name, e, r0, kt, c0, n, rows, halved = spec
            w = I[name][0] if e is None else I[name][0, e]
            if name in LORA:
                view = w[r0:r0 + rows, :].rearrange("p (k n) -> p k n", k=2)
            else:
                view = w[r0:r0 + 128 * kt, c0:c0 + n].rearrange("(k p) n -> p k n", p=128)
            j = len(P.issued)
            s = j % len(P.raw)

            def at(buf):
                return buf.rearrange("p (k n) -> p k n", k=2)[0:rows, 0:kt, 0:n]

            dst = at(P.raw[s])
            free = P.slot_free[s]
            P.q["sp"].append((lambda g: g.dma_start(dst, view), [free] if free else [], (P.slot_sem[s], 16)))
            tok = (P.slot_sem[s], 16 * (j // len(P.raw) + 1))
            if not halved:
                P.issued.append((s, None, dst, None, tok))
                return
            z = P.halves % len(P.hi)
            P.halves += 1
            hi, lo = at(P.hi[z]), at(P.lo[z])
            t = P.act(lambda g: g.activation(hi, dst, ACT.Copy), tok, P.half_free[z])
            t = P.dve(lambda g: g.tensor_tensor(lo, dst, hi.bitcast(F32), ALU.subtract), t, P.half_free[z])
            P.slot_free[s] = t
            P.issued.append((s, z, hi, lo, t))

        def piece(name, e, r0, kt, c0, n, rows=128, halved=True):
            spec = (name, e, r0, kt, c0, n, rows, halved)
            j = len(P.specs)
            P.specs.append(spec)
            if len(P.issued) == j:
                issue(spec)
            assert not P.ahead or P.ahead[j] == spec
            while len(P.issued) <= j + P.look and len(P.issued) < len(P.ahead):
                issue(P.ahead[len(P.issued)])
            return P.issued[j]

        def used(pc, t):
            if pc[1] is None:
                P.slot_free[pc[0]] = t
            else:
                P.half_free[pc[1]] = t

        def finish():
            if plan is None:
                return

            with nc.Block() as block:
                @block.sync
                def _(e):
                    P.emit("sp", e)

                @block.tensor
                def _(e):
                    P.emit("pe", e)

                @block.vector
                def _(e):
                    P.emit("dve", e)

                @block.scalar
                def _(e):
                    P.emit("act", e)

                @block.gpsimd
                def _(e):
                    P.emit("pool", e)

        ident = alloc(128)
        shiftd = alloc(128)
        carry = alloc(128)
        ucent = alloc(128)
        tri_inc = alloc(128)
        tri_str = alloc(128)
        invm_at = top[0]
        invm = alloc(7 * 128).rearrange("p (l t) -> p l t", l=7)
        cmask = alloc(128)
        ones = alloc(128)
        cols = alloc(4)
        CD = math.exp(-0.5)

        def asel(o, i, op, fill, base, pattern, cm):
            return P.pool(lambda g: g.affine_select(out=o, in_=i, compare_op=op, fill=fill, base=base,
                                                    pattern=pattern, channel_multiplier=cm))

        P.pool(lambda g: g.memset(ones, 1.0))
        one = ones[:, 0:128]
        P.pool(lambda g: g.memset(ident, 0.0))
        asel(ident, ident, ALU.not_equal, 1.0, 0, [[-1, 128]], 1)
        P.pool(lambda g: g.memset(shiftd, 0.0))
        asel(shiftd, shiftd, ALU.not_equal, 1.0, 1, [[-1, 128]], 1)
        asel(shiftd, shiftd, ALU.not_equal, -1.0, 0, [[-1, 128]], 1)
        P.pool(lambda g: g.memset(carry, 0.0))
        asel(carry, carry, ALU.not_equal, 1.0, -127, [[128, 128]], 1)
        asel(tri_inc, one, ALU.is_ge, 0.0, 0, [[1, 128]], -1)
        asel(tri_str, one, ALU.is_gt, 0.0, 0, [[1, 128]], -1)
        P.pool(lambda g: g.memset(ucent, -CD))
        asel(ucent, ucent, ALU.is_ge, 0.0, 0, [[1, 128]], -1)
        t_c = P.pool(lambda g: g.tensor_scalar(ucent[0:64, :], ucent[0:64, :], CD, None, ALU.add))
        for l in range(7):
            b = 1 << l
            m = invm[:, l, :]
            P.pool(lambda g, m=m: g.memset(m, 0.0))
            v = m.rearrange("p (n h r) -> p n h r", h=2, r=b)[:, :, 1, :]
            o1 = ones[:, 0:64].rearrange("p (n r) -> p n r", r=b)
            asel(v, o1, ALU.is_ge, 0.0, 0, [[-2 * b, 64 // b], [0, b]], 1)
            asel(v, v, ALU.is_gt, 0.0, b, [[2 * b, 64 // b], [0, b]], -1)
        P.pool(lambda g: g.memset(cmask, 0.0))
        asel(cmask, cmask, ALU.is_ge, NEG, 0, [[-1, 128]], 1)
        P.pool(lambda g: g.memset(cols, -CD))
        asel(cols[:, 0:1], cols[:, 0:1], ALU.is_gt, 0.0, -63, [[0, 1]], 1)
        asel(cols[:, 1:2], cols[:, 1:2], ALU.is_gt, 0.0, 64, [[0, 1]], -1)
        P.pool(lambda g: g.memset(cols[:, 2:3], 0.0))
        twice = alloc(64)
        P.pool(lambda g: g.memset(twice, 0.0))
        asel(twice, twice, ALU.not_equal, 1.0, 0, [[-1, 64]], 1)
        t_const = asel(twice, twice, ALU.not_equal, 1.0, -64, [[-1, 64]], 1)

        def selector():
            sel = alloc(16 * 128).rearrange("p (h t) -> p h t", h=16)
            P.pool(lambda g: g.memset(sel, 0.0))
            return sel, asel(sel, sel, ALU.not_equal, 1.0, 0, [[-1, 16], [0, 128]], 1)


        x = tm(2048)
        mark_x = top[0]
        t_x = P.loads([(x, I["x"][0].rearrange("(b p) d -> p b d", p=128))], e="act")

        def copy(e, o, i, *after, scale=None):
            if e == "act":
                return P.act(lambda g: g.activation(o, i, ACT.Copy, scale=1.0 if scale is None else scale), *after)
            if scale is None:
                return P.dve(lambda g: g.tensor_copy(o, i), *after)
            return P.dve(lambda g: g.tensor_scalar(o, i, scale, None, ALU.mult), *after)

        def rcp(o, i, *after):
            return P.dve(lambda g: g.reciprocal(o, i), *after)

        def mset(o, value):
            return P.dve(lambda g: g.memset(o, value))

        def tt(o, a, b, op, *after):
            return P.dve(lambda g: g.tensor_tensor(o, a, b, op), *after)

        def ts(o, a, s1, s2, o1, o2=None, *after):
            if o2 is None:
                return P.dve(lambda g: g.tensor_scalar(o, a, s1, None, o1), *after)
            return P.dve(lambda g: g.tensor_scalar(o, a, s1, s2, o1, o2), *after)

        def stt(o, a, s, b, o1, o2, *after):
            return P.dve(lambda g: g.scalar_tensor_tensor(out=o, in0=a, scalar=s, in1=b, op0=o1, op1=o2), *after)

        def actf(o, i, f, *after, bias=None, scale=1.0):
            if bias is None:
                return P.act(lambda g: g.activation(o, i, f, scale=scale), *after)
            return P.act(lambda g: g.activation(o, i, f, bias=bias, scale=scale), *after)

        def red(o, i, op, *after):
            return P.dve(lambda g: g.tensor_reduce(o, i, AX.X, op), *after)

        def mm(o, l, r, start, stop, *after, sig=False):
            return P.pe(lambda g: g.matmul(o, l, r, start=start, stop=stop, skip_group_check=True), *after, sig=sig)

        def tr(o, i, *after, sig=False):
            k = i.shape[0]
            return P.pe(lambda g: g.transpose(o, i, ident[0:k, 0:k]), *after, sig=sig)

        def to_fm(src, dst, C, *after):
            toks = [None, None]
            for j in range(C // 512):
                i, ps, free = pair()
                v = ps.rearrange("p (b k t) -> p b k t", b=2, k=4)
                for b in range(2):
                    for k in range(4):
                        t = tr(v[:, b, k, :], src[:, b, 512 * j + 128 * k:512 * j + 128 * k + 128],
                               *((free + after) if b == 0 and k == 0 else ()), sig=(b == 1 and k == 3))
                d = dst[:, 4 * j:4 * j + 4, :].rearrange("p k (b t) -> p b k t", b=2)
                toks[j % 2] = copy("act" if j % 2 else "dve", d, v, t)
                done(i, toks[j % 2])
            return tuple(t for t in toks if t)

        def to_halves(src, hl, C, *after):
            for j in range(C // 512):
                i, ps, free = pair()
                v = ps.rearrange("p (b k t) -> p b k t", b=2, k=4)
                for b in range(2):
                    for k in range(4):
                        t = tr(v[:, b, k, :], src[:, b, 512 * j + 128 * k:512 * j + 128 * k + 128],
                               *((free + after) if b == 0 and k == 0 else ()), sig=(b == 1 and k == 3))
                dh, dl = [z[:, 4 * j:4 * j + 4, :].rearrange("p k (b t) -> p b k t", b=2) for z in hl]
                t = P.act(lambda g, dh=dh, v=v: g.activation(dh, v, ACT.Copy), t)
                t = P.dve(lambda g, dh=dh, dl=dl, v=v: g.tensor_tensor(dl, v, dh.bitcast(F32), ALU.subtract), t)
                done(i, t)
            return (t,)

        def halve(src, hi, lo, *after):
            t = P.act(lambda g: g.activation(hi, src, ACT.Copy), *after)
            return P.dve(lambda g: g.tensor_tensor(lo, src, hi.bitcast(F32), ALU.subtract), t)

        def fm_r(k):
            return [alloc_r(k * 256).rearrange("p (k t) -> p k t", t=256) for _ in range(2)]

        def proj_a(xT, KT, wn, c0, ncols, consume, *after, bias=None, e=None):
            split = isinstance(xT, list)
            for ci, c in enumerate(range(0, ncols, 512)):
                n = min(512, ncols - c)
                i, ps, free = pair()
                v = ps.rearrange("p (b n) -> p b n", b=2)[:, :, 0:n]
                first = free + after
                if bias is not None:
                    for b in range(2):
                        mm(v[:, b, :], ones[0:1, 0:128], bias[0:1, c:c + n], True, False, *first)
                        first = ()
                for g0 in range(0, KT, 2):
                    pc = piece(wn, e, 128 * g0, 2, c0 + c, n, halved=split)
                    _, _, hi, lo, tok = pc
                    for b in range(2):
                        tb = slice(128 * b, 128 * b + 128)
                        for k in range(2):
                            st, sp = bias is None and g0 + k == 0, g0 + k == KT - 1
                            if split:
                                xh, xl = xT[0][:, g0 + k, tb], xT[1][:, g0 + k, tb]
                                mm(v[:, b, :], xh, hi[:, k, :], st, False, tok, *first)
                                mm(v[:, b, :], xh, lo[:, k, :], False, False)
                                t = mm(v[:, b, :], xl, hi[:, k, :], False, sp, sig=(b == 1 and k == 1))
                            else:
                                t = mm(v[:, b, :], xT[:, g0 + k, tb], hi[:, k, :], st, sp, tok, *first,
                                       sig=(b == 1 and k == 1))
                            first = ()
                    used(pc, t)
                done(i, *consume(ci, n, v, t))

        def proj_b(xT, KT, wn, c0, ncols, consume, *after):
            split = isinstance(xT, list)
            for ci in range(ncols // 512):
                c = c0 + 512 * ci
                i, ps, free = pair()
                v = ps.rearrange("p (m t) -> p m t", m=4)
                first = free + after
                for g0 in range(0, KT, 2):
                    pc = piece(wn, None, 128 * g0, 2, c, 512, halved=split)
                    _, _, hi, lo, tok = pc
                    for m in range(4):
                        cm = slice(128 * m, 128 * m + 128)
                        for k in range(2):
                            st, sp = g0 + k == 0 and m % 2 == 0, g0 + k == KT - 1
                            if split:
                                xh, xl = xT[0][:, g0 + k, :], xT[1][:, g0 + k, :]
                                mm(v[:, m, :], hi[:, k, cm], xh, st, False, tok, *first)
                                mm(v[:, m, :], hi[:, k, cm], xl, False, False)
                                t = mm(v[:, m, :], lo[:, k, cm], xh, False, sp, sig=(m == 3 and k == 1))
                            else:
                                t = mm(v[:, m, :], hi[:, k, cm], xT[:, g0 + k, :], st, sp, tok, *first,
                                       sig=(m == 3 and k == 1))
                            first = ()
                    used(pc, t)
                done(i, *consume(ci, v, t))

        def dump(v, *after):
            o = out[0].rearrange("(b p) d -> p b d", p=128)
            t = P.loads([(o[:, :, 0:v.shape[2]], v)], *after, e="act")
            P.q["act"].append((None, [t], None))
            finish()
            return planned

        xT_at = top[0]
        xT = fm_r(16)
        t_xT = to_halves(x, xT, 2048, t_x, t_const)
        mark0 = top[0]

        P.barrier()
        UR = tm(3360)
        A1, A2 = [x.rearrange("p b c -> p (b c)")[:, 2048 * k:2048 * k + 2048].rearrange("p (b c) -> p b c", b=2)
                  for k in range(2)]
        a3 = alloc(2048)
        A3 = a3.rearrange("p (b c) -> p b c", b=2)
        PB, QB, RB, BB = tm(1024), tm(1024), tm(1024), tm(1024)
        fmbase = top[0]
        turned = alloc(2048)
        aT, bT, cT, rT = [turned[:, 512 * k:512 * k + 512].rearrange("p (q t) -> p q t", q=4) for k in range(4)]
        mats = top[0]
        room = alloc(3072)
        LT, X, XT, T1, LB = [z.rearrange("p (h t) -> p h t", h=8) for z in (
            a3[:, 0:1024], a3[:, 1024:2048], room[:, 0:1024], room[:, 1024:2048], room[:, 2048:3072])]
        loraT = alloc(1280).rearrange("p (k t) -> p k t", t=256)
        nmv, nu, nh, nht = [alloc(512) for _ in range(4)]
        small = alloc(256)
        kstate = alloc(8 * 64).rearrange("p (i v) -> p i v", i=8)
        pz = alloc(8)
        mub = at(fmbase, 3360)
        par = room.rearrange("p (k c) -> p k c", k=3)
        rows = at(mats + 3072 + 1280, 2048)[0:1, :]
        t_mu = P.loads([(mub, I["mu_shift"][0].partition_broadcast(128)),
                        (rows[:, 0:1024], I["w0"]), (rows[:, 1024:2048], I["a0"])])

        def eat_ur(ci, n, ps, t):
            d = UR[:, :, 512 * ci:512 * ci + n]
            t1 = copy("act", d, ps, t)
            i, p2, free = pair()
            v = p2.rearrange("p (b n) -> p b n", b=2)[:, :, 0:n]
            mm(v[:, 0, :], shiftd, d[:, 0, :], True, True, t1, *free)
            mm(v[:, 1, :], shiftd, d[:, 1, :], True, False)
            t2 = mm(v[:, 1, :], carry, d[:, 0, :], False, True, sig=True)
            mb = mub[:, 512 * ci:512 * ci + n].unsqueeze(1).broadcast_to([128, 2, n])
            t3 = tt(v, v, mb, ALU.mult, t2, t_mu)
            t4 = tt(d, d, v, ALU.add, t3)
            done(i, t4)
            return (t1,)

        proj_a(xT, 16, "w_in", 0, 3360, eat_ur, *t_xT)
        t_par = P.loads([(par[:, 0, :], I["k_k"][0].partition_broadcast(128)),
                         (par[:, 1, :], I["k_a"][0].partition_broadcast(128)),
                         (par[:, 2, :], I["r_k"][0].rearrange("h n -> (h n)").partition_broadcast(128))],
                        P.last("dve"))
        r_, k_, v_ = [UR[:, :, 1024 * i:1024 * i + 1024] for i in range(3)]
        lo = UR[:, :, 3072:3360]
        t_l = actf(lo[:, :, 0:64], lo[:, :, 0:64], ACT.Tanh, P.last("dve"))
        t_l = actf(lo[:, :, 128:288], lo[:, :, 128:288], ACT.Sigmoid)
        i, ps, free = pair()
        pv = ps.rearrange("p (k t) -> p k t", t=256)
        i2, ps2, free2 = pair()
        pv2 = ps2.rearrange("p (k t) -> p k t", t=256)
        for b in range(2):
            tb = slice(128 * b, 128 * b + 128)
            tr(pv[0:64, 0, tb], lo[:, b, 0:64], t_l, *(free if b == 0 else ()))
            tr(pv[0:64, 1, tb], lo[:, b, 64:128])
            tr(pv[:, 2, tb], lo[:, b, 128:256])
            t = tr(pv2[0:32, 0, tb], lo[:, b, 256:288], *(free2 if b == 0 else ()), sig=True)
        copy("dve", loraT[0:64, 0:2, :], pv[0:64, 0:2, :], t)
        copy("dve", loraT[:, 2, :], pv[:, 2, :])
        t_lT = copy("dve", loraT[0:32, 3, :], pv2[0:32, 0, :])
        done(i, t_lT)
        done(i2, t_lT)

        def lora(wname, row, parts, consume):
            sls = []
            r0 = 0
            for (kk_, rr) in parts:
                pc = piece(wname, None, r0, 2, 0, 512, rows=rr, halved=False)
                sls.append((pc, pc[2], pc[4], kk_, rr))
                r0 += rr
            for c in range(2):
                i, ps, free = pair()
                v = ps.rearrange("p (b n) -> p b n", b=2)
                first = free + (t_lT, t_mu)
                for b in range(2):
                    st = True
                    if row is not None:
                        mm(v[:, b, :], ones[0:1, 0:128], row[:, 512 * c:512 * c + 512], True, False, *first)
                        first, st = (), False
                    for j, (s, sl, tok, kk_, rr) in enumerate(sls):
                        t = mm(v[:, b, :], loraT[0:rr, kk_, 128 * b:128 * b + 128], sl[:, c, :], st,
                               j == len(sls) - 1, tok, *first, sig=(b == 1 and j == len(sls) - 1))
                        first, st = (), False
                done(i, consume(c, v, t))
            for pc, *_ in sls:
                used(pc, t)

        sig_ = A1
        lora("w_w2", rows[:, 0:1024], [(0, 64)],
             lambda c, v, t: actf(sig_[:, :, 512 * c:512 * c + 512], v, ACT.Sigmoid, t))
        lora("w_a2", rows[:, 1024:2048], [(1, 64)],
             lambda c, v, t: actf(A2[:, :, 512 * c:512 * c + 512], v, ACT.Sigmoid, t))
        t_sig = P.last("act")
        t_dec = None
        for c in range(2):
            cs = slice(512 * c, 512 * c + 512)
            i, ps, free = pair()
            v = ps.rearrange("p (b n) -> p b n", b=2)
            mm(v[:, 0, :], ucent, sig_[:, 0, cs], True, True, t_sig, *free)
            t = mm(v[:, 1, :], ucent, sig_[:, 1, cs], True, True, sig=True)
            actf(PB[:, :, cs], v, ACT.Exp, t)
            t1 = actf(QB[:, :, cs], v, ACT.Exp, scale=-1.0)
            t2 = stt(v, sig_[:, :, cs], CD, v, ALU.mult, ALU.add, t1)
            t_dec = actf(RB[:, :, cs], v, ACT.Exp, t2)
            done(i, t_dec)
        i, ps, free = pair()
        for j in range(8):
            mm(ps[:, j:j + 1], sig_[:, 0, 128 * j:128 * j + 128], cols[:, 0:1], True, False, *(free if j == 0 else ()))
            t = mm(ps[:, j:j + 1], sig_[:, 1, 128 * j:128 * j + 128], cols[:, 1:2], False, True, sig=(j == 7))
        t_pz = actf(pz, ps[:, 0:8], ACT.Exp, t)
        done(i, t_pz)
        kk = A3

        def hd(v):
            return v.rearrange("p b (h n) -> p b h n", n=64)

        def pb(k):
            return par[:, k, :].unsqueeze(1).broadcast_to([128, 2, 1024])

        sm = small.rearrange("p (k b h) -> p k b h", k=8, b=2)
        tt(kk, k_, pb(0), ALU.mult, t_par)
        tt(BB, kk, kk, ALU.mult)
        for b in range(2):
            t = red(sm[:, 0, b, :], hd(BB)[:, b], ALU.add)
        t = actf(sm[:, 1], sm[:, 0], ACT.Sqrt, t)
        ts(sm[:, 1], sm[:, 1], 1e-12, None, ALU.max, None, t)
        rcp(sm[:, 2], sm[:, 1])
        for b in range(2):
            rk = sm[:, 2, b, :].unsqueeze(2).broadcast_to([128, 16, 64])
            tt(hd(kk)[:, b], hd(kk)[:, b], rk, ALU.mult)
        aa = A2
        stt(BB, aa, -1.0, pb(1), ALU.add, ALU.mult)
        stt(k_, BB, 1.0, k_, ALU.add, ALU.mult)
        tt(BB, r_, k_, ALU.mult)
        tt(BB, BB, pb(2), ALU.mult)
        for b in range(2):
            red(sm[:, 3, b, :], hd(BB)[:, b], ALU.add)
        tt(BB, aa, kk, ALU.mult)
        tt(BB, BB, QB, ALU.mult, t_dec)
        tt(QB, QB, k_, ALU.mult)
        tt(RB, RB, kk, ALU.mult)
        t_sc = tt(PB, PB, r_, ALU.mult)
        Y = A1
        t_all = P.last("act")
        for b in range(2):
            tb = slice(128 * b, 128 * b + 128)
            for hg in range(2):
                for two in range(2):
                    i, ps, free = pair()
                    for j in range(8):
                        src = (RB, BB, QB, PB)[2 * two + j // 4]
                        t = tr(ps[:, 128 * j:128 * j + 128],
                               src[:, b, 512 * hg + 128 * (j % 4):512 * hg + 128 * (j % 4) + 128],
                               *((t_sc,) + free if j == 0 else ()), sig=(j == 7))
                    t_fm = copy("dve", turned[:, 1024 * two:1024 * two + 1024], ps, t)
                    done(i, t_fm)
                def head(par_, q):
                    return 8 * hg + 2 * q + par_

                def grid(lf, rf, o, after, mask=None, scale=None, e="dve"):
                    i, ps, free = pair()
                    v = ps.rearrange("p (h t) -> p h t", h=8)
                    for par_ in range(2):
                        for q in range(4):
                            j = 4 * par_ + q
                            t = mm(v[:, j, :], lf(par_, q), rf(par_, q), True, True,
                                   *((free + after) if j == 0 else ()), sig=(j == 7))
                    if mask is not None:
                        mb = mask.unsqueeze(1).broadcast_to([128, 8, 128])
                        t = tt(o, v, mb, ALU.mult, t)
                    else:
                        t = copy(e, o, v, t)
                    done(i, t)
                    return t

                def row(T):
                    return lambda par_, q: T[64 * par_:64 * par_ + 64, q, :]

                t_lt = grid(row(bT), row(aT), LT, (t_fm,), mask=tri_str)
                idb = ident.unsqueeze(1).broadcast_to([128, 8, 128])

                def lower(l, *after):
                    mb = invm[:, l, :].unsqueeze(1).broadcast_to([128, 8, 128])
                    return P.pool(lambda g: g.tensor_tensor(LB, LT, mb, ALU.mult), *after)

                t = tt(XT, idb, LB, ALU.subtract, lower(0, t_lt))
                i, ps, free = pair()
                v = ps.rearrange("p (h t) -> p h t", h=8)
                t_x = [None, None]
                for a_ in range(2):
                    h4 = slice(4 * a_, 4 * a_ + 4)
                    for q in range(4):
                        t1 = tr(v[:, 4 * a_ + q, :], XT[:, 4 * a_ + q, :], *((t,) + free if a_ + q == 0 else ()),
                                sig=(q == 3))
                    t_x[a_] = copy("act", X[:, h4, :], v[:, h4, :], t1)
                done(i, *t_x)
                t_lb = lower(1, t)
                for l in range(1, 7):
                    i, ps, free = pair()
                    v = ps.rearrange("p (h t) -> p h t", h=8)
                    t_t1 = [None, None]
                    for a_ in range(2):
                        h4 = slice(4 * a_, 4 * a_ + 4)
                        for q in range(4):
                            t = mm(v[:, 4 * a_ + q, :], LB[:, 4 * a_ + q, :], X[:, 4 * a_ + q, :], True, True,
                                   *((t_lb, t_x[a_]) + free if q == 0 else ()), sig=(q == 3))
                        t_t1[a_] = copy("act", T1[:, h4, :], v[:, h4, :], t)
                    done(i, *t_t1)
                    if l < 6:
                        t_lb = lower(l + 1, t)
                    for a_ in range(2):
                        h4 = slice(4 * a_, 4 * a_ + 4)
                        i, ps, free = pair()
                        for q in range(4):
                            j = 4 * a_ + q
                            mm(ps[:, 128 * q:128 * q + 128], XT[:, j, :], T1[:, j, :], True, True,
                               *((t_t1[a_],) + free if q == 0 else ()))
                            t = mm(ps[:, 512 + 128 * q:640 + 128 * q], T1[:, j, :], XT[:, j, :], True, True, sig=(q == 3))
                        t1 = tt(X[:, h4, :], X[:, h4, :], ps[:, 0:512].rearrange("p (h t) -> p h t", h=4),
                                ALU.subtract, t)
                        t_x[a_] = tt(XT[:, h4, :], XT[:, h4, :], ps[:, 512:1024].rearrange("p (h t) -> p h t", h=4),
                                     ALU.subtract)
                        done(i, t_x[a_])
                t_m = grid(row(cT), row(aT), T1, (), mask=tri_str)
                t_r1 = grid(row(cT), row(rT), LB, (), mask=tri_inc)
                t_r2 = grid(row(bT), row(rT), LT, (), mask=tri_inc)
                vh = v_[:, b, :].rearrange("p (h n) -> p h n", n=64)
                nmv8, nu8, nh8 = [z.rearrange("p (h n) -> p h n", n=64) for z in (nmv, nu, nh)]
                nht4 = nht.rearrange("p (q t) -> p q t", q=4)

                def grid64(lf, rf, o, after, scale=None, e="dve"):
                    i, ps, free = pair()
                    v = ps[:, 0:512].rearrange("p (h n) -> p h n", h=8)
                    for j in range(8):
                        t = mm(v[:, j, :], lf(j // 4, j % 4), rf(j // 4, j % 4), True, True,
                               *((free + after) if j == 0 else ()), sig=(j == 7))
                    t = copy(e, o, v, t, scale=scale)
                    done(i, t)
                    return t

                t_mv = grid64(lambda a_, q: T1[:, 4 * a_ + q, :], lambda a_, q: vh[:, head(a_, q), :], nmv8,
                              (t_m, P.last("pe")), scale=-1.0)
                t_u = grid64(lambda a_, q: XT[:, 4 * a_ + q, :], lambda a_, q: nmv8[:, 4 * a_ + q, :], nu8, (t_mv,))
                alh = RB[:, b, :].rearrange("p (h n) -> p h n", n=64)
                if b == 1:
                    t_h = grid64(lambda a_, q: XT[:, 4 * a_ + q, :], lambda a_, q: alh[:, head(a_, q), :],
                                 nh.rearrange("p (q a n) -> p a q n", q=4, a=2), (), scale=-1.0)
                    i, ps, free = pair()
                    v = ps[:, 0:512].rearrange("p (q t) -> p q t", q=4)
                    for q in range(4):
                        t = tr(v[:, q, :], nh[:, 128 * q:128 * q + 128], *((t_h,) + free if q == 0 else ()), sig=(q == 3))
                    t_ht = copy("dve", nht4, v, t)
                    done(i, t_ht)
                    i, ps, free = pair()
                    for a_ in range(2):
                        for q in range(4):
                            o = ps[:, 512 * a_ + 64 * q:512 * a_ + 64 * q + 64]
                            t = mm(o, nht4[64 * a_:64 * a_ + 64, q, :], kstate[64 * a_:64 * a_ + 64, 4 * hg + q, :],
                                   True, True, *((t_ht,) + free if a_ + q == 0 else ()), sig=(a_ + q == 4))
                    for a_ in range(2):
                        t_u = tt(nu8[:, 4 * a_:4 * a_ + 4, :], nu8[:, 4 * a_:4 * a_ + 4, :],
                                 ps[:, 512 * a_:512 * a_ + 256].rearrange("p (q n) -> p q n", q=4), ALU.add, t)
                    done(i, t_u)
                i, ps, free = pair()
                first = free + (t_u, t_r1, t_r2)
                for a_ in range(2):
                    for q in range(4):
                        o = ps[:, 512 * a_ + 64 * q:512 * a_ + 64 * q + 64]
                        st = True
                        if b == 1:
                            mm(o, rT[64 * a_:64 * a_ + 64, q, :],
                               kstate[64 * a_:64 * a_ + 64, 4 * hg + q, :], True, False, *first)
                            st, first = False, ()
                        mm(o, LB[:, 4 * a_ + q, :], vh[:, head(a_, q), :], st, False, *first)
                        first = ()
                        t = mm(o, LT[:, 4 * a_ + q, :], nu8[:, 4 * a_ + q, :], False, True, sig=(a_ + q == 4))
                for a_ in range(2):
                    yo = Y[:, b, 512 * hg:512 * hg + 512].rearrange("p (q a n) -> p a q n", q=4, a=2)[:, a_]
                    t_y = copy("dve", yo, ps[:, 512 * a_:512 * a_ + 256].rearrange("p (q n) -> p q n", q=4), t)
                done(i, t_y)
                if b == 0:
                    i, ps, free = pair()
                    kh, bh = [z[:, 0, :].rearrange("p (h n) -> p h n", n=64) for z in (QB, BB)]
                    for a_ in range(2):
                        for q in range(4):
                            o = ps[64 * a_:64 * a_ + 64, 512 * a_ + 64 * q:512 * a_ + 64 * q + 64]
                            mm(o, kh[:, head(a_, q), :], vh[:, head(a_, q), :], True, False,
                               *(free if a_ + q == 0 else ()))
                            t = mm(o, bh[:, head(a_, q), :], nu8[:, 4 * a_ + q, :], False, True, sig=(a_ + q == 4))
                    for a_ in range(2):
                        pa = slice(64 * a_, 64 * a_ + 64)
                        pzb = pz[pa, 4 * hg:4 * hg + 4].unsqueeze(2).broadcast_to([64, 4, 64])
                        t_z = tt(kstate[pa, 4 * hg:4 * hg + 4, :],
                                 ps[pa, 512 * a_:512 * a_ + 256].rearrange("p (q n) -> p q n", q=4),
                                 pzb, ALU.mult, t, t_pz)
                    done(i, t_z)
                P.pending["pe"] = P.pending["pe"] + [P.last("dve")]
        t_ln = P.loads([(A3[:, 0, :], I["lnx_w"][0].partition_broadcast(128)),
                        (A3[:, 1, :], I["lnx_b"][0].partition_broadcast(128))], P.last("dve"), P.last("pe"))
        G = A2
        lora("w_g2", None, [(2, 128), (3, 32)],
             lambda c, v, t: copy("act", G[:, :, 512 * c:512 * c + 512], v, t, t_sc))
        t_g = P.last("act")

        def head_norm(y, tmp, s, nh_, n, eps):
            yh = y.rearrange("p b (h n) -> p b h n", n=n)
            th = tmp.rearrange("p b (h n) -> p b h n", n=n)
            for b in range(2):
                red(s[:, 0, b, :], yh[:, b], ALU.add)
            ts(s[:, 0], s[:, 0], 1.0 / n, None, ALU.mult)
            for b in range(2):
                tt(yh[:, b], yh[:, b], s[:, 0, b, :].unsqueeze(2).broadcast_to([128, nh_, n]), ALU.subtract)
            tt(tmp, y, y, ALU.mult)
            for b in range(2):
                red(s[:, 1, b, :], th[:, b], ALU.add)
            t = ts(s[:, 1], s[:, 1], 1.0 / n, eps, ALU.mult, ALU.add)
            t = actf(s[:, 2], s[:, 1], ACT.Sqrt, t)
            rcp(s[:, 3], s[:, 2], t)
            for b in range(2):
                tt(yh[:, b], yh[:, b], s[:, 3, b, :].unsqueeze(2).broadcast_to([128, nh_, n]), ALU.mult)

        head_norm(Y, PB, sm[:, 4:8], 16, 64, 64e-5)
        tt(Y, Y, A3[:, 0, :].unsqueeze(1).broadcast_to([128, 2, 1024]), ALU.mult, t_ln)
        tt(Y, Y, A3[:, 1, :].unsqueeze(1).broadcast_to([128, 2, 1024]), ALU.add)
        for b in range(2):
            tt(hd(PB)[:, b], hd(v_)[:, b], sm[:, 3, b, :].unsqueeze(2).broadcast_to([128, 16, 64]), ALU.mult)
        tt(Y, Y, PB, ALU.add)
        t_yr = tt(Y, Y, G, ALU.mult, t_g)
        yrT = at(mark0, 2048).rearrange("p (k t) -> p k t", t=256)
        P.barrier()
        t_yrT = to_fm(Y, yrT, 1024, t_yr)
        P.barrier()
        top[0] = mark0 + 2048

        qk, qc, qs = fm(8), fm(8), fm(8)
        vm, om, hm, tmp = tm(1024), tm(1024), tm(1024), tm(1024)
        cw = alloc(40).rearrange("p (j k) -> p j k", j=5)
        rw = alloc(8 * 256).rearrange("p (k t) -> p k t", t=256)
        rr = alloc(6 * 128).rearrange("p (b k t) -> p b k t", b=2, k=3)
        gb = alloc(4)
        colz = alloc(48).rearrange("p (b k h) -> p b k h", b=2, k=3)
        E = alloc(1024).rearrange("p (h t) -> p h t", h=8)
        kg = alloc(512)
        cst = alloc(4 * 129).rearrange("p (q v) -> p q v", q=4)
        sm2 = alloc(8 * 16).rearrange("p (k b h) -> p k b h", k=8, b=2)
        mhw = alloc(1024)
        t_p = P.loads([(cw, I["conv"]), (gb[0:8, 0:1], I["i_bias"].rearrange("o h -> h o")),
                       (gb[0:8, 1:2], I["f_bias"].rearrange("o h -> h o")),
                       (mhw, I["mh_w"][0].partition_broadcast(128))])

        proj_b(xT, 16, "w_in", 3360, 1024, lambda ci, v, t: (copy("act", qk[:, 4 * ci:4 * ci + 4, :], v, t),))
        t_qk = P.last("act")
        proj_a(xT, 16, "w_in", 4384, 1024, lambda ci, n, v, t: (copy("act", vm[:, :, 512 * ci:512 * ci + n], v, t),))
        t_v = P.last("act")
        sel, t_sel = selector()

        def rows_of(wn, c0, parts, *after):
            g16 = alloc(32).rearrange("p (b n) -> p b n", b=2)
            proj_a(xT, 16, wn, c0, 16, lambda ci, n, v, t: (copy("dve", g16, v, t),), *after)
            t = P.last("dve")
            i, ps, free = pair()
            for u, (a, n) in enumerate(parts):
                for b in range(2):
                    t1 = tr(ps[0:n, 512 * u + 128 * b:512 * u + 128 * b + 128], g16[:, b, a:a + n],
                            *((t,) + free if u + b == 0 else ()), sig=(b == 1))
            return i, ps, t1

        i, ps, t = rows_of("w_in", 5408, ((0, 8), (8, 8)))
        R = [rw[0:8, k, :] for k in range(8)]
        ts(R[0], ps[0:8, 0:256], gb[0:8, 0:1], None, ALU.add, None, t, t_p)
        t = ts(R[1], ps[0:8, 512:768], gb[0:8, 1:2], None, ALU.add)
        done(i, t)

        def log_sigmoid(f, s, o, after=()):
            t = stt(s, f, -1.0, f, ALU.mult, ALU.max, *after)
            t = actf(s, s, ACT.Exp, t, scale=-1.0)
            t = actf(s, s, ACT.Ln, bias=ones[0:s.shape[0], 0:1])
            return stt(o, f, 0.0, s, ALU.min, ALU.subtract, t)

        log_sigmoid(R[1], R[2], R[3])
        mset(R[7], 1.0)

        def scan(o, d0, d1, init, o0, o1, *after):
            return P.dve(lambda g: g.tensor_tensor_scan(o, d0, d1, init, o0, o1), *after)

        for b in range(2):
            tb = slice(128 * b, 128 * b + 128)
            scan(R[4][:, tb], R[7][:, tb], R[3][:, tb], 0.0, ALU.mult, ALU.add)
            tt(R[5][:, tb], R[0][:, tb], R[4][:, tb], ALU.subtract)
            if b == 0:
                scan(R[6][:, tb], R[5][:, tb], R[5][:, tb], -3e38, ALU.max, ALU.max)
                tt(gb[0:8, 2:3], R[4][:, 127:128], R[6][:, 127:128], ALU.add)
                ts(gb[0:8, 3:4], R[6][:, 127:128], -1.0, None, ALU.mult)
            else:
                scan(R[6][:, tb], R[5][:, tb], R[5][:, tb], gb[0:8, 2:3], ALU.max, ALU.max)
            copy("dve", rr[0:8, b, 0, :], R[5][:, tb])
            t = tt(rr[0:8, b, 1, :], R[4][:, tb], R[6][:, tb], ALU.add)
            actf(rr[0:8, b, 1, :], rr[0:8, b, 1, :], ACT.Exp, t, scale=-1.0)
            if b == 0:
                t_rr = actf(rr[0:8, 0, 2, :], R[5][:, tb], ACT.Exp, bias=gb[0:8, 3:4])
            else:
                t_rr = actf(rr[0:8, 1, 2, :], R[6][:, tb], ACT.Exp, scale=-1.0, bias=gb[0:8, 2:3])
        i, ps, free = pair()
        for b in range(2):
            for k in range(3):
                t = tr(ps[:, 24 * b + 8 * k:24 * b + 8 * k + 8], rr[0:8, b, k, :],
                       *((t_rr,) + free if b + k == 0 else ()), sig=(b + k == 3))
        t = copy("dve", colz, ps[:, 0:48].rearrange("p (b k h) -> p b k h", b=2, k=3), t)
        done(i, t)
        for j in range(8):
            ts(qc[:, j, :], qk[:, j, :], cw[:, 3, j:j + 1], cw[:, 4, j:j + 1], ALU.mult, ALU.add, t_qk, t_p)
            for d in range(1, 4):
                stt(qc[:, j, d:256], qk[:, j, 0:256 - d], cw[:, 3 - d, j:j + 1], qc[:, j, d:256], ALU.mult, ALU.add)
        t = actf(qs, qc, ACT.Sigmoid, P.last("dve"))
        tt(qs[:, 0:4, :], qs[:, 0:4, :], qc[:, 0:4, :], ALU.mult, t)
        t_qs = stt(qs[:, 4:8, :], qs[:, 4:8, :], 0.125, qc[:, 4:8, :], ALU.mult, ALU.mult)
        proj_a(xT, 16, "w_in", 5424, 1024, lambda ci, n, v, t: (
            actf(om[:, :, 512 * ci:512 * ci + n], v, ACT.Sigmoid, t),))
        t_o = P.last("act")
        vh = vm.rearrange("p b (h n) -> p b h n", n=128)
        hh = hm.rearrange("p b (h n) -> p b h n", n=128)

        def hsel(j):
            return 2 * (j % 4) + j // 4

        for b in range(2):
            tb = slice(128 * b, 128 * b + 128)
            i, ps, free = pair()
            v = ps.rearrange("p (h t) -> p h t", h=8)
            for j in range(8):
                t = mm(v[:, j, :], sel[0:8, hsel(j), :], R[6][:, tb], True, True,
                       *((P.last("dve"), t_sel) + free if j == 0 else ()), sig=(j == 7))
            for j in range(8):
                g_ = colz[:, b, 0, hsel(j):hsel(j) + 1]
                t1 = ts(E[:, j, :], v[:, j, :], g_, 0.0, ALU.subtract, ALU.max, t)
            done(i, t1)
            t = actf(E, E, ACT.Exp, t1, scale=-1.0)
            tt(E, E, tri_inc.unsqueeze(1).broadcast_to([128, 8, 128]), ALU.mult, t)
            i, ps, free = pair()
            v = ps.rearrange("p (h t) -> p h t", h=8)
            for j in range(8):
                pa, q = slice(64 * (j // 4), 64 * (j // 4) + 64), j % 4
                t = mm(v[:, j, :], qs[pa, 4 + q, tb], qs[pa, q, tb], True, True,
                       *((t_qs,) + free if j == 0 else ()), sig=(j == 7))
            t_e = tt(E, E, v, ALU.mult, t)
            done(i, t_e)
            i, ps, free = pair()
            v = ps.rearrange("p (h n) -> p h n", h=8)
            i2, ps2, free2 = pair()
            for j in range(8):
                h = hsel(j)
                mm(v[:, h, :], E[:, j, :], vh[:, b, h, :], True, True, *((t_e, t_v) + free if j == 0 else ()))
                t = mm(ps2[:, h:h + 1], E[:, j, :], ones[:, 0:1], True, True, *(free2 if j == 0 else ()), sig=(j == 7))
            copy("dve", hh[:, b], v, t)
            t = copy("dve", sm2[:, 0, b, :], ps2[:, 0:8])
            done(i, t)
            done(i2, t)
            if b == 1:
                i, ps, free = pair()
                i2, ps2, free2 = pair()
                for j in range(8):
                    pa, q = slice(64 * (j // 4), 64 * (j // 4) + 64), j % 4
                    mm(ps[:, 128 * j:128 * j + 128], qs[pa, q, tb], cst[pa, q, 0:128], True, True,
                       *((P.last("dve"),) + free if j == 0 else ()))
                    t = mm(ps2[:, 512 * (j // 4) + q:512 * (j // 4) + q + 1], qs[pa, q, tb], cst[pa, q, 128:129],
                           True, True, *(free2 if j == 0 else ()), sig=(j == 7))
                for j in range(8):
                    h = hsel(j)
                    stt(hh[:, 1, h, :], ps[:, 128 * j:128 * j + 128], colz[:, 1, 2, h:h + 1], hh[:, 1, h, :],
                        ALU.mult, ALU.add, t)
                    o = 512 * (j // 4) + j % 4
                    t1 = stt(sm2[:, 0, 1, h:h + 1], ps2[:, o:o + 1], colz[:, 1, 2, h:h + 1],
                             sm2[:, 0, 1, h:h + 1], ALU.mult, ALU.add)
                done(i, t1)
                done(i2, t1)
            stt(sm2[:, 1, b, :], sm2[:, 0, b, :], -1.0, sm2[:, 0, b, :], ALU.mult, ALU.max)
            tt(sm2[:, 1, b, :], sm2[:, 1, b, :], colz[:, b, 1, :], ALU.max)
            rcp(sm2[:, 2, b, :], sm2[:, 1, b, :])
            tt(hh[:, b], hh[:, b], sm2[:, 2, b, :].unsqueeze(2).broadcast_to([128, 8, 128]), ALU.mult)
            if b == 0:
                i, ps, free = pair()
                for q in range(4):
                    t = tr(ps[:, 128 * q:128 * q + 128], qs[:, 4 + q, 0:128], *((P.last("dve"),) + free if q == 0 else ()),
                           sig=(q == 3))
                gz = colz[:, 0, 2, :].unsqueeze(2).broadcast_to([128, 8, 64])
                t_kg = tt(kg.rearrange("p (h n) -> p h n", n=64), ps[:, 0:512].rearrange("p (h n) -> p h n", n=64),
                          gz, ALU.mult, t)
                done(i, t_kg)
                i, ps, free = pair()
                i2, ps2, free2 = pair()
                for j in range(8):
                    h = hsel(j)
                    pa, q = slice(64 * (j // 4), 64 * (j // 4) + 64), j % 4
                    mm(ps[pa, 512 * (j // 4) + 128 * q:512 * (j // 4) + 128 * q + 128], kg[:, 64 * h:64 * h + 64],
                       vh[:, 0, h, :], True, True, *((t_kg,) + free if j == 0 else ()))
                    t = mm(ps2[pa, 512 * (j // 4) + q:512 * (j // 4) + q + 1], kg[:, 64 * h:64 * h + 64], ones[:, 0:1],
                           True, True, *(free2 if j == 0 else ()), sig=(j == 7))
                for a_ in range(2):
                    pa = slice(64 * a_, 64 * a_ + 64)
                    copy("dve", cst[pa, :, 0:128], ps[pa, 512 * a_:512 * a_ + 512].rearrange("p (q n) -> p q n", q=4), t)
                    t1 = copy("dve", cst[pa, :, 128:129], ps2[pa, 512 * a_:512 * a_ + 4].unsqueeze(2))
                done(i, t1)
                done(i2, t1)
        head_norm(hm, tmp, sm2[:, 4:8], 8, 128, 1e-6)
        tt(hm, hm, mhw.unsqueeze(1).broadcast_to([128, 2, 1024]), ALU.mult)
        t_ym = tt(hm, hm, om, ALU.mult, t_o)
        ymT = qk
        t_ymT = to_fm(hm, ymT, 1024, t_ym)
        P.barrier()
        o0 = mark0 + 2048 + 2048
        mix = at(o0, 4096).rearrange("p (b c) -> p b c", b=2)
        gs = [at(o0 + 4096 + 1024 * k, 1024).rearrange("p (b c) -> p b c", b=2) for k in range(2)]
        top[0] = o0 + 6144
        bgr = alloc(4096)
        t_p = P.loads([(bgr[0:1, :], I["b_gate"])])
        for c in range(4):
            cs = slice(512 * c, 512 * c + 512)
            for k, (goff, yT, wb) in enumerate(((6448, yrT, "w_br"), (8496, ymT, "w_bm"))):
                proj_a(xT, 16, "w_in", goff + 512 * c, 512,
                       lambda ci, n, v, t, k=k: (actf(gs[k], v, ACT.Sigmoid, t, P.last("dve")),), t_p,
                       bias=bgr[:, 2048 * k + 512 * c:2048 * k + 512 * c + 512])
                tg = P.last("act")

                def eat(ci, n, v, t, k=k, cs=cs, tg=tg):
                    if k == 0:
                        return (tt(mix[:, :, cs], gs[0], v, ALU.mult, t, tg),)
                    t = tt(gs[1], gs[1], v, ALU.mult, t, tg)
                    tt(mix[:, :, cs], mix[:, :, cs], gs[1], ALU.add)
                    return (t,)

                proj_a(yT, 8, wb, 512 * c, 512, eat)
        P.barrier()
        t_x = P.loads([(x, I["x"][0].rearrange("(b p) d -> p b d", p=128))])
        mixT = xT
        t_mixT = to_halves(mix, mixT, 2048)
        res = x

        def eat_out(res, alpha):
            def f(ci, n, v, t):
                cs = slice(512 * ci, 512 * ci + n)
                return (stt(res[:, :, cs], res[:, :, cs], alpha, v, ALU.mult, ALU.add, t),)
            return f

        P.pending["dve"] = P.pending["dve"] + [t_x]
        proj_a(mixT, 16, "w_out", 0, 2048, eat_out(res, ALPHA), *t_mixT)

        def layer_norm(v, wn, bn, wt, bt, st, *after):
            t_w = P.loads([(wt, I[wn][0].partition_broadcast(128)), (bt, I[bn][0].partition_broadcast(128))], *after)
            for b in range(2):
                s6 = st[:, 24 * b:24 * b + 24]
                for c in range(4):
                    P.dve(lambda g, b=b, c=c, s6=s6: g.bn_stats(s6[:, 6 * c:6 * c + 6], v[:, b, 512 * c:512 * c + 512]))
                P.dve(lambda g, b=b, s6=s6: g.bn_aggr(st[:, 48 + 2 * b:50 + 2 * b], s6))
                t = ts(st[:, 52 + b:53 + b], st[:, 49 + 2 * b:50 + 2 * b], 1e-5, None, ALU.add)
                t = actf(st[:, 54 + b:55 + b], st[:, 52 + b:53 + b], ACT.Sqrt, t)
                rcp(st[:, 56 + b:57 + b], st[:, 54 + b:55 + b], t)
                ts(v[:, b, :], v[:, b, :], st[:, 48 + 2 * b:49 + 2 * b], st[:, 56 + b:57 + b], ALU.subtract, ALU.mult)
                tt(v[:, b, :], v[:, b, :], wt, ALU.mult, t_w)
                t = tt(v[:, b, :], v[:, b, :], bt, ALU.add)
            return t

        P.barrier()
        top[0] = mark0
        wt, bt, st = alloc(2048), alloc(2048), alloc(64)
        t_x1 = layer_norm(x, "ln1_w", "ln1_b", wt, bt, st)
        x1T = xT
        t_x1T = to_halves(x, x1T, 2048, t_x1)
        P.barrier()
        top[0] = mark0

        wr = alloc(16 * 36).rearrange("p (k n) -> p k n", k=16)
        br = alloc(36)
        wg = alloc(64).rearrange("p (b e) -> p b e", b=2)
        asg = alloc(64).rearrange("p (b e) -> p b e", b=2)
        rs = alloc(2 * 160).rearrange("p (b n) -> p b n", b=2)
        t_r = P.loads([(wr[:, :, 0:4], I["w_rg"][0].rearrange("(k p) n -> p k n", p=128)),
                       (wr[:, :, 4:36], I["w_re"][0].rearrange("(k p) n -> p k n", p=128)),
                       (br[0:1, 0:4], I["b_rg"]), (br[0:1, 4:36], I["b_re"])])
        wrh, wrl = [alloc_r(16 * 36).rearrange("p (k n) -> p k n", k=16) for _ in range(2)]
        t_wr = halve(wr, wrh, wrl, t_r)
        i, ps, free = pair()
        for b in range(2):
            o = ps[:, 512 * b:512 * b + 36]
            tb = slice(128 * b, 128 * b + 128)
            mm(o, ones[0:1, 0:128], br[0:1, :], True, False, t_wr, *(free if b == 0 else ()))
            for k in range(16):
                mm(o, x1T[0][:, k, tb], wrh[:, k, :], False, False)
                mm(o, x1T[1][:, k, tb], wrh[:, k, :], False, False)
                t = mm(o, x1T[0][:, k, tb], wrl[:, k, :], False, k == 15, sig=(k == 15))
        for b in range(2):
            s = rs[:, b, :]
            lg, le0 = s[:, 0:4], s[:, 4:36]
            copy("dve", s[:, 0:36], ps[:, 512 * b:512 * b + 36], t)
            if b == 1:
                done(i, P.last("dve"))

            def first_max(l, n, m, o, s1):
                red(m, l, ALU.max)
                ts(s1[:, 1:1 + n], l, m, None, ALU.is_ge)
                mset(s1[:, 0:1], 0.0)
                scan(s1[:, 1:1 + n], s1[:, 1:1 + n], s1[:, 1:1 + n], 0.0, ALU.max, ALU.max)
                return tt(o, s1[:, 1:1 + n], s1[:, 0:n], ALU.subtract)

            gm, og, nm, ex, gw = s[:, 36:37], s[:, 37:41], s[:, 41:42], s[:, 42:46], s[:, 46:47]
            scr = s[:, 48:60]
            first_max(lg, 4, gm, og, scr)
            t1 = ts(nm, gm, -1.0, None, ALU.mult)
            t1 = actf(ex, lg, ACT.Exp, t1, bias=nm)
            red(gw, ex, ALU.add, t1)
            rcp(gw, gw)
            le, o1, le2, o2 = s[:, 60:68], s[:, 68:76], s[:, 76:84], s[:, 84:92]
            m1, m2, w1, w2 = s[:, 92:93], s[:, 93:94], s[:, 94:95], s[:, 95:96]
            ts(le, le0[:, 0:8], og[:, 0:1], None, ALU.mult)
            for g_ in range(1, 4):
                stt(le, le0[:, 8 * g_:8 * g_ + 8], og[:, g_:g_ + 1], le, ALU.mult, ALU.add)
            first_max(le, 8, m1, o1, scr)
            stt(le2, o1, NEG, le, ALU.mult, ALU.add)
            first_max(le2, 8, m2, o2, scr)
            t1 = tt(w2, m2, m1, ALU.subtract)
            t1 = actf(w2, w2, ACT.Exp, t1)
            ts(w1, w2, 1.0, None, ALU.add, None, t1)
            rcp(w1, w1)
            tt(w1, w1, gw, ALU.mult)
            tt(w2, w2, w1, ALU.mult)
            tt(asg[:, b, 0:8], o1, o2, ALU.add)
            ts(o1, o1, w1, None, ALU.mult)
            stt(o1, o2, w2, o1, ALU.mult, ALU.add)
            for g_ in (3, 2, 1, 0):
                ts(asg[:, b, 8 * g_:8 * g_ + 8], asg[:, b, 0:8], og[:, g_:g_ + 1], None, ALU.mult)
            for g_ in range(4):
                t_wg = ts(wg[:, b, 8 * g_:8 * g_ + 8], o1, og[:, g_:g_ + 1], None, ALU.mult)

        rm = alloc(64).rearrange("p (b e) -> p b e", b=2)
        over = alloc(64).rearrange("p (b e) -> p b e", b=2)
        wover = alloc(64).rearrange("p (b e) -> p b e", b=2)
        iota = alloc(64)
        fl = alloc(4)
        i, ps, free = pair()
        mm(ps[:, 0:32], tri_str, asg[:, 0, :], True, True, P.last("dve"), *free)
        mm(ps[:, 32:64], tri_str, asg[:, 1, :], True, False)
        t = mm(ps[:, 32:64], ones[:, 0:128], asg[:, 0, :], False, True, sig=True)
        stt(rm, ps[:, 0:64].rearrange("p (b e) -> p b e", b=2), 1.0, asg, ALU.add, ALU.mult, t)
        done(i, P.last("dve"))
        ts(rm, rm, -1.0, None, ALU.add)
        ts(over, rm, CAP - 0.5, None, ALU.is_ge)
        tt(wover, over, wg, ALU.mult)
        red(fl[:, 0:1], over.rearrange("p b e -> p (b e)"), ALU.add)
        i, ps, free = pair()
        t = mm(ps[0:1, 0:1], fl[:, 0:1], ones[:, 0:1], True, True, P.last("dve"), *free, sig=True)
        flag = fl[0:1, 1:2].bitcast(mybir.dt.int32)
        t_flag = ts(flag, ps[0:1, 0:1], 1.0, None, ALU.min, None, t)
        done(i, t_flag)
        scan(iota, ones[:, 0:64], ones[:, 0:64], -1.0, ALU.mult, ALU.add)
        if CAP < 64:
            mset(iota[:, CAP:64], -5.0)

        xm = [alloc_r(4096).rearrange("p (b c) -> p b c", b=2) for _ in range(2)]
        t_xm = halve(x, xm[0], xm[1])
        acc = x
        ts(acc, x, ALPHA, None, ALU.mult)
        free_from = top[0]
        xg = [alloc_r(2048).rearrange("p (k s) -> p k s", k=16) for _ in range(2)]
        yb = [alloc(2048) for _ in range(2)]
        hs = [alloc_r(512).rearrange("p (f s) -> p f s", f=4) for _ in range(2)]
        gu = alloc(1024)
        sgm = alloc(256).rearrange("p (f s) -> p f s", f=4)
        sel_ = [alloc_r(128).rearrange("p (b s) -> p b s", b=2) for _ in range(2)]
        selw, selT = [[alloc(256).rearrange("p (b s) -> p b s", b=2) for _ in range(m)] for m in (2, 4)]
        t_xg, t_selT, t_y, t_hs = {}, {}, {}, {}

        t_sel, t_sc = {}, {}

        def select(e):
            z = e % 2
            for b in range(2):
                ts(sel_[z][:, b, :], iota, rm[:, b, e:e + 1], None, ALU.is_equal, None, t_sel.get(e - 2))
                for a_ in range(2):
                    t = ts(selw[z][:, b, 64 * a_:64 * a_ + 64], iota, rm[:, b, e:e + 1], wg[:, b, e:e + 1],
                           ALU.is_equal, ALU.mult)
            t_sel[e] = t

        def gather(e, hf):
            z = e % 2
            t = t_sel[e]
            i, ps, free = pair()
            v = ps.rearrange("p (k s) -> p k s", k=8)
            for k in range(8):
                d0 = 128 * (8 * hf + k)
                for a_ in range(2):
                    for b in range(2):
                        t1 = mm(v[:, k, 64 * a_:64 * a_ + 64], xm[a_][:, b, d0:d0 + 128], sel_[z][:, b, :],
                                b == 0, b == 1, *((t, t_xm) + free if k + b + a_ == 0 else ()),
                                sig=(k == 7 and b + a_ == 2))
                if k < 7:
                    yield
            t1 = copy("act", xg[z][:, 8 * hf:8 * hf + 8, :], v, t1)
            done(i, t1)
            t_xg[e] = t1
            if hf == 1:
                i, ps, free = pair()
                for b in range(2):
                    t1 = tr(ps[:, 128 * b:128 * b + 128], selw[z][:, b, :], *(free if b == 0 else ()), sig=(b == 1))
                t_sel[e] = t1
                t_selT[e] = copy("dve", selT[e % 4], ps[:, 0:256].rearrange("p (b s) -> p b s", b=2), t1, t_sc.get(e - 4))
                done(i, t_selT[e])
            yield

        def drain(g):
            for _ in g:
                pass

        def gate_up(e, fill):
            i, ps, free = pair()
            for u, wn in enumerate(("w_gate", "w_up")):
                o = ps[:, 512 * u:512 * u + 512]
                for g0 in range(0, 16, 2):
                    pc = piece(wn, e, 128 * g0, 2, 0, 512)
                    _, _, hi, lo, tok = pc
                    for k in range(2):
                        l = xg[e % 2][:, g0 + k, :]
                        mm(o, l, hi[:, k, :], g0 + k == 0, False, tok, t_xg[e], *(free if u + g0 + k == 0 else ()))
                        t = mm(o, l, lo[:, k, :], False, g0 + k == 15, sig=(k == 1))
                    used(pc, t)
                    if g0 or u:
                        next(fill, None)
            t_gu = copy("act", gu, ps, t)
            done(i, t_gu)
            return t_gu

        def hidden(e, t_gu):
            i, ps, free = pair()
            for u in range(2):
                for f in range(4):
                    o = ps[:, 512 * u + 64 * f:512 * u + 64 * f + 64]
                    t = mm(o, gu[:, 512 * u + 128 * f:512 * u + 128 * f + 128], twice, True, True,
                           *((t_gu,) + free if u + f == 0 else ()), sig=(u + f == 4))
            vg, vu = [ps[:, 512 * u:512 * u + 256].rearrange("p (f s) -> p f s", f=4) for u in range(2)]
            t = actf(sgm, vg, ACT.Sigmoid, t, t_hs.get(e - 1))
            tt(sgm, sgm, vg, ALU.mult, t)
            t = tt(sgm, sgm, vu, ALU.mult)
            done(i, t)
            t_hs[e] = halve(sgm, hs[e % 2][:, :, 0:64], hs[e % 2][:, :, 64:128], t)

        def downs(e):
            for hf in range(2):
                i, ps, free = pair()
                for c in range(2):
                    o = ps[:, 512 * c:512 * c + 512]
                    for g0 in range(0, 4, 2):
                        pc = piece("w_down", e, 128 * g0, 2, 512 * (2 * hf + c), 512)
                        _, _, hi, lo, tok = pc
                        for k in range(2):
                            l = hs[e % 2][:, g0 + k, :]
                            mm(o, l, hi[:, k, :], g0 + k == 0, False, tok, t_hs[e], *(free if c + g0 + k == 0 else ()))
                            t = mm(o, l, lo[:, k, :], False, g0 + k == 3, sig=(k == 1))
                        used(pc, t)
                t_y[e] = copy("act", yb[e % 2][:, 1024 * hf:1024 * hf + 1024], ps, t)
                done(i, t_y[e])

        def scatter(e):
            for c in range(4):
                i, ps, free = pair()
                v = ps.rearrange("p (b n) -> p b n", b=2)
                for b in range(2):
                    t = mm(v[:, b, :], selT[e % 4][:, b, :], yb[e % 2][:, 512 * c:512 * c + 512], True, True,
                           *((t_y[e], t_selT[e]) + free if b == 0 else ()), sig=(b == 1))
                    if b == 0:
                        yield
                a4 = acc[:, :, 512 * c:512 * c + 512]
                done(i, tt(a4, a4, v, ALU.add, t))
                yield
            t_sc[e] = t

        def work(e):
            for n in range(8):
                if e < 31:
                    next(g0, None)
                yield
                if e:
                    next(sc_, None)
                yield

        select(0)
        drain(gather(0, 0))
        drain(gather(0, 1))
        for e in range(32):
            sc_ = scatter(e - 1) if e else iter(())
            if e < 31:
                select(e + 1)
                g0, g1 = gather(e + 1, 0), gather(e + 1, 1)
            else:
                g0 = g1 = iter(())
            t_gu = gate_up(e, work(e))
            drain(g0)
            drain(sc_)
            hidden(e, t_gu)
            drain(g1)
            downs(e)
        drain(scatter(31))

        main = P
        assert main.pe_signed
        all_done = [main.last(o) for o in ("pe", "dve", "act", "pool")]
        top[0] = free_from
        P = Prog(nc, ctx, "r", alloc_bufs(2, 1), plans.get("r", []), 0)
        planned["r"] = P.specs
        sg, hb, hT = tm(512), tm(512), fm_r(4)

        def down(e, toks):
            def eat(ci, n, v, t):
                cs = slice(512 * ci, 512 * ci + 512)
                for b in range(2):
                    t1 = stt(acc[:, b, cs], v[:, b, :], wover[:, b, e:e + 1], acc[:, b, cs], ALU.mult, ALU.add, t)
                return (t1,)

            proj_a(hT, 4, "w_down", 0, 2048, eat, *toks, e=e)

        for e in range(32):
            proj_a(x1T, 16, "w_gate", 0, 512,
                   lambda ci, n, v, t: (actf(sg, v, ACT.Sigmoid, t, P.last("dve")),
                                        tt(sg, sg, v, ALU.mult, P.last("act"))), e=e)
            proj_a(x1T, 16, "w_up", 0, 512, lambda ci, n, v, t: (tt(hb, sg, v, ALU.mult, t),), e=e)
            down(e, to_halves(hb, hT, 512, P.last("dve")))
        rest, P = P, main
        for o in ("pe", "dve", "act", "sp", "pool"):
            P.q[o].append(((flag, rest), (t_flag, all_done), None))
        P.barrier()
        top[0] = free_from
        pt = tm(256)
        pT = fm(2)
        gs = tm(512)
        t_pl = P.loads([(pt, I["p"][0, 0].rearrange("(b p) d -> p b d", p=128))])
        i, ps, free = pair()
        v = ps.rearrange("p (k b t) -> p k b t", k=4, b=2)
        for b in range(2):
            for k in range(2):
                t = tr(v[:, k, b, :], pt[:, b, 128 * k:128 * k + 128], *((t_pl,) + free if b + k == 0 else ()),
                       sig=(b + k == 2))
        t_pT = copy("dve", pT.rearrange("p k (b t) -> p k b t", b=2), v[:, 0:2], t)
        done(i, t_pT)
        for c in range(4):
            cs = slice(512 * c, 512 * c + 512)
            proj_a(x1T, 16, "w_pg", 512 * c, 512,
                   lambda ci, n, v, t: (actf(gs, v, ACT.Sigmoid, t, P.last("dve")),))

            def eat(ci, n, v, t, cs=cs):
                t = tt(gs, gs, v, ALU.mult, t, P.last("act"))
                tt(acc[:, :, cs], acc[:, :, cs], gs, ALU.add)
                return (t,)

            proj_a(pT, 2, "w_ple", 512 * c, 512, eat, t_pT)
        P.barrier()
        top[0] = mark0
        wt, bt, st = alloc(2048), alloc(2048), alloc(64)
        t_x2 = layer_norm(x, "ln2_w", "ln2_b", wt, bt, st)

        def rms(v, gsrc, o, wt, st, *after):
            t_w = P.loads([(wt, gsrc.partition_broadcast(128))], *after)
            for b in range(2):
                tt(o[:, b, :], v[:, b, :], v[:, b, :], ALU.mult)
                red(st[:, b:b + 1], o[:, b, :], ALU.add)
                t = ts(st[:, 2 + b:3 + b], st[:, b:b + 1], 1.0 / 2048, 1e-6, ALU.mult, ALU.add)
                t = actf(st[:, 4 + b:5 + b], st[:, 2 + b:3 + b], ACT.Sqrt, t)
                rcp(st[:, 6 + b:7 + b], st[:, 4 + b:5 + b], t)
                t = stt(o[:, b, :], v[:, b, :], st[:, 6 + b:7 + b], wt, ALU.mult, ALU.mult, t_w)
            return t

        P.barrier()
        top[0] = mark0
        markh = top[0]
        hT_ = xT
        hn = tm(2048)
        wt, st = alloc(2048), alloc(64)
        t_h = rms(x, I["norm_even_g_2"][0], hn, wt, st)
        t_hT_ = to_halves(hn, hT_, 2048, t_h)
        P.barrier()
        top[0] = markh
        oT = fm(16)
        uT, zb = fm(8), fm(8)
        mark_s5 = top[0]
        qT, kT, za = fm(8), fm(8), fm(8)
        vv = tm(1024)
        bw = alloc(4096).rearrange("p (h x) -> p h x", h=16)
        scs = [alloc(1536), at(xT_at, 1536)]
        pr = alloc(1536).rearrange("p (j t) -> p j t", j=12)
        mxs = [alloc(32).rearrange("p (k b h) -> p k b h", k=4, b=2) for _ in range(2)]
        t_bw = P.loads([(bw, I["bias_windows"])])
        proj_b(hT_, 16, "w_in_even_2", 0, 1024, lambda ci, v, t: (copy("act", qT[:, 4 * ci:4 * ci + 4, :], v, t, scale=0.125),),
               *t_hT_)
        proj_b(hT_, 16, "w_in_even_2", 1024, 1024, lambda ci, v, t: (copy("act", kT[:, 4 * ci:4 * ci + 4, :], v, t),))
        proj_a(hT_, 16, "w_in_even_2", 2048, 1024, lambda ci, n, v, t: (copy("act", vv[:, :, 512 * ci:512 * ci + n], v, t),))
        proj_b(hT_, 16, "w_in_even_2", 3072, 1024, lambda ci, v, t: (copy("act", uT[:, 4 * ci:4 * ci + 4, :], v, t),))

        def silu_into(dst):
            def f(ci, v, t):
                d = dst[:, 4 * ci:4 * ci + 4, :]
                t1 = actf(d, v, ACT.Sigmoid, t)
                return (tt(d, d, v, ALU.mult, t1),)
            return f

        proj_b(hT_, 16, "w_in_even_2", 4096, 1024, silu_into(za))
        proj_b(hT_, 16, "w_in_even_2", 5120, 1024, silu_into(zb))
        t_qkv = P.last("act")
        t_za = P.last("dve")

        def softmax_exp(u):
            sc, mx = scs[u % 2], mxs[u % 2]
            s4 = sc.rearrange("p (h x) -> p h x", h=4)
            parts = (s4[:, :, 0:128], s4[:, :, 128:384])
            for b in range(2):
                n = 128 * (b + 1)
                red(mx[:, 0, b, :], parts[b], ALU.max)
                tt(parts[b], parts[b], mx[:, 0, b, :].unsqueeze(2).broadcast_to([128, 4, n]), ALU.subtract)
            return actf(sc, sc, ACT.Exp, P.last("dve"))

        def softmax_turn(u, t):
            sc, mx = scs[u % 2], mxs[u % 2]
            s4 = sc.rearrange("p (h x) -> p h x", h=4)
            parts = (s4[:, :, 0:128], s4[:, :, 128:384])
            for b in range(2):
                n = 128 * (b + 1)
                red(mx[:, 1, b, :], parts[b], ALU.add, t)
                rcp(mx[:, 2, b, :], mx[:, 1, b, :])
                t1 = tt(parts[b], parts[b], mx[:, 2, b, :].unsqueeze(2).broadcast_to([128, 4, n]), ALU.mult)
            toks = []
            for half in range(2):
                i, ps, free = pair()
                for j in range(6):
                    m = 6 * half + j
                    off = 512 * (j // 3) + 128 * (j % 3)
                    t = tr(ps[:, off:off + 128], sc[:, 128 * m:128 * m + 128], *((t1,) + free if j == 0 else ()),
                           sig=(j == 5))
                t = copy("act", pr[:, 6 * half:6 * half + 6, :].rearrange("p (a k) t -> p a k t", a=2),
                         ps.rearrange("p (a x) -> p a x", a=2)[:, :, 0:384].rearrange("p a (k t) -> p a k t", k=3),
                         t, P.last("pe"))
                done(i, t)
            return t

        def even_scores(u):
            i, ps, free = pair()
            i2, ps2, free2 = pair()
            pp = (ps, ps2)
            for j in range(4):
                h = 4 * u + j
                pa, q = slice(64 * (h % 2), 64 * (h % 2) + 64), h // 2
                o = pp[j % 2][:, 512 * (j // 2):512 * (j // 2) + 384]
                mm(o[:, 0:128], qT[pa, q, 0:128], kT[pa, q, 0:128], True, True,
                   *(free + (t_qkv,) if j == 0 else free2 if j == 1 else ()))
                t = mm(o[:, 128:384], qT[pa, q, 128:256], kT[pa, q, 0:256], True, True, sig=(j == 3))
            s4 = scs[u % 2].rearrange("p (h x) -> p h x", h=4)
            for j in range(4):
                o = pp[j % 2][:, 512 * (j // 2):512 * (j // 2) + 384]
                bwh = bw[:, 4 * u + j, :]
                tt(s4[:, j, 0:128], o[:, 0:128], bwh[:, 128:256], ALU.add, t, t_bw, P.last("pe"))
                t1 = tt(s4[:, j, 128:384], o[:, 128:384], bwh, ALU.add)
            done(i, t1)
            done(i2, t1)
            mset(s4[0:64, :, 64:128], NEG)
            mset(s4[0:64, :, 320:384], NEG)
            return softmax_exp(u)

        keep, top[0] = top[0], xT_at + 1536
        lr, li, ld = alloc(32), alloc(32), alloc(32)
        bre, bim, cre, cim = [alloc(512).rearrange("p (i c) -> p i c", i=32) for _ in range(4)]
        dsk, bgl = alloc(8), alloc(8)
        V = [alloc(32) for _ in range(14)]
        Bb = [alloc(512).rearrange("p (i c) -> p i c", i=32) for _ in range(3)]
        phases = [[alloc(1024).rearrange("p (i t) -> p i t", i=4) for _ in range(2)], [None, None]]
        assert top[0] <= xT_at + 8192 and keep <= TOT - 1024
        top[0] = keep
        scratch = [at(TOT - 1024 + 512 * k, 512).rearrange("p (i t) -> p i t", i=4) for k in range(2)]
        t_s = P.loads([(lr, I["s5_lr"]), (li, I["s5_li"]),
                       (ld[0:64, :], I["s5_ld"][0].partition_broadcast(64)),
                       (ld[64:128, :], I["s5_ld"][1].partition_broadcast(64)),
                       (bre, I["s5_bre"]), (bim, I["s5_bim"]), (cre, I["s5_cre"]), (cim, I["s5_cim"]),
                       (dsk, I["s5_dd"]), (bgl, I["bglu"])], P.last("pe"), P.last("dve"), P.last("act"))
        dt, mag, ang, k2, sn, cs_, are, aim, den, cr, ci_, tA, tB, tC = V

        def s5_setup():
            actf(dt, ld, ACT.Exp, t_s)
            t = tt(mag, lr, dt, ALU.mult, P.last("act"))
            t = actf(mag, mag, ACT.Exp, t)
            tt(ang, li, dt, ALU.mult, t)
            TP = 2 * math.pi
            C1 = 6.28125
            C2 = 2029.0 / 2 ** 20
            C3 = TP - C1 - C2
            MG = 12582912.0
            ts(k2, ang, 1.0 / TP, MG, ALU.mult, ALU.add)
            ts(k2, k2, -MG, None, ALU.add)
            stt(ang, k2, -C1, ang, ALU.mult, ALU.add)
            stt(ang, k2, -C2, ang, ALU.mult, ALU.add)
            stt(ang, k2, -C3, ang, ALU.mult, ALU.add)
            PI = 3.1415925
            ts(sn, ang, PI, -PI, ALU.min, ALU.max)
            ts(cs_, ang, math.pi / 2, None, ALU.add)
            ts(tA, cs_, PI, -TP, ALU.is_gt, ALU.mult)
            tt(cs_, cs_, tA, ALU.add)
            ts(cs_, cs_, PI, -PI, ALU.min, ALU.max)
            actf(sn, sn, ACT.Sin, P.last("dve"))
            t = actf(cs_, cs_, ACT.Sin)
            tt(are, mag, cs_, ALU.mult, t)
            tt(aim, mag, sn, ALU.mult)
            tt(tA, lr, lr, ALU.mult)
            tt(tB, li, li, ALU.mult)
            tt(den, tA, tB, ALU.add)
            rcp(den, den)
            ts(are, are, -1.0, None, ALU.add)
            tt(tA, are, lr, ALU.mult)
            tt(tB, aim, li, ALU.mult)
            tt(tA, tA, tB, ALU.add)
            tt(cr, tA, den, ALU.mult)
            tt(tA, aim, lr, ALU.mult)
            tt(tB, are, li, ALU.mult)
            tt(tA, tA, tB, ALU.subtract)
            tt(ci_, tA, den, ALU.mult)
            crb = cr.unsqueeze(2).broadcast_to([128, 32, 16])
            cib = ci_.unsqueeze(2).broadcast_to([128, 32, 16])
            tt(Bb[0], bre, crb, ALU.mult)
            tt(Bb[2], bim, cib, ALU.mult)
            tt(Bb[0], Bb[0], Bb[2], ALU.subtract)
            tt(Bb[1], bim, crb, ALU.mult)
            tt(Bb[2], bre, cib, ALU.mult)
            tt(Bb[1], Bb[1], Bb[2], ALU.add)
            ts(cim, cim, -1.0, None, ALU.mult)
            t_ab = P.last("dve")
            return t_ab

        def ptt(o, a, b, op, *after):
            return P.pool(lambda g: g.tensor_tensor(o, a, b, op), *after)

        def make_phases(j, t_free, t_ab=None):
            CC, SS = phases[j % 2]
            j4 = slice(4 * j, 4 * j + 4)
            P.pool(lambda g: g.memset(CC[:, :, 0:1], 1.0), t_free, t_ab)
            P.pool(lambda g: g.memset(SS[:, :, 0:1], 0.0))
            P.pool(lambda g: g.tensor_copy(CC[:, :, 1:2], cs_[:, j4].unsqueeze(2)))
            P.pool(lambda g: g.tensor_copy(SS[:, :, 1:2], sn[:, j4].unsqueeze(2)))
            for l in range(8):
                n = 1 << l
                w = min(n, 255 - n)
                src = slice(1, 1 + w)
                dst = slice(n + 1, n + 1 + w)
                cb = CC[:, :, n:n + 1].broadcast_to([128, 4, w])
                sb_ = SS[:, :, n:n + 1].broadcast_to([128, 4, w])
                A, B = [z[:, :, 0:w] for z in scratch]
                ptt(A, CC[:, :, src], cb, ALU.mult)
                ptt(B, SS[:, :, src], sb_, ALU.mult)
                ptt(CC[:, :, dst], A, B, ALU.subtract)
                ptt(A, CC[:, :, src], sb_, ALU.mult)
                ptt(B, SS[:, :, src], cb, ALU.mult)
                t = ptt(SS[:, :, dst], A, B, ALU.add)
            return t

        t_e = even_scores(0)
        for u in range(4):
            t_now = t_e
            if u < 3:
                t_e = even_scores(u + 1)
            if u == 1:
                t_ph = [make_phases(0, None, s5_setup())]
            t_pr = softmax_turn(u, t_now)
            i, ps, free = pair()
            for j in range(4):
                h = 4 * u + j
                o = ps[64 * (j % 2):64 * (j % 2) + 64, 512 * (j // 2):512 * (j // 2) + 256]
                mm(o, vv[:, 0, 64 * h:64 * h + 64], pr[:, 3 * j:3 * j + 2, :].rearrange("p a t -> p (a t)"), True, False,
                   *(free + (t_pr,) if j == 0 else ()))
                t = mm(o[:, 128:256], vv[:, 1, 64 * h:64 * h + 64], pr[:, 3 * j + 2, :], False, True, sig=(j == 3))
            t = tt(oT[:, 2 * u:2 * u + 2, :], ps.rearrange("p (a x) -> p a x", a=2)[:, :, 0:256],
                   za[:, 2 * u:2 * u + 2, :], ALU.mult, t, t_za)
            done(i, t)

        P.barrier()
        top[0] = mark_s5
        pads = [alloc(640) for _ in range(4)]
        BT = [alloc(512).rearrange("p (i c) -> p i c", i=4) for _ in range(2)]
        phases[1][:] = [alloc(1024).rearrange("p (i t) -> p i t", i=4) for _ in range(2)]
        MM = [[alloc(1024).rearrange("p (i t) -> p i t", i=4) for _ in range(2)] for _ in range(2)]
        Z1, Z2 = [alloc(1024).rearrange("p (i t) -> p i t", i=4) for _ in range(2)]
        gz = alloc(256)
        yT = fm(8)
        assert top[0] <= TOT - 1024
        for z in pads:
            mset(z, 0.0)
        def pad(j, zs, srcs, *after):
            for z, src in zip(zs, srcs):
                d = z.rearrange("p (i x) -> p i x", i=4)
                for hf in range(2):
                    pa = slice(64 * hf, 64 * hf + 64)
                    t = P.dve(lambda g, d=d, src=src, pa=pa, hf=hf, j=j: g.tensor_copy(
                        d[pa, :, 16 * hf:16 * hf + 16], src[pa, 4 * j:4 * j + 4, :]), *after)
            return t

        def turn_b(t_pd):
            got = []
            for z in range(2):
                i, ps, free = pair()
                for q in range(4):
                    t = tr(ps[:, 128 * q:128 * q + 128], pads[z][:, 128 * q:128 * q + 128],
                           *((t_pd,) + free if q == 0 else ()), sig=(q == 3))
                got.append((i, ps, t))
            return got

        def b_times_u(j, got):
            for z, (i, ps, t) in enumerate(got):
                t_bt = copy("dve", BT[z], ps[:, 0:512].rearrange("p (i c) -> p i c", i=4), t)
                done(i, t_bt)
            i, ps, free = pair()
            i2, ps2, free2 = pair()
            br_, bi_ = [z.rearrange("p (i t) -> p i t", i=4) for z in (ps, ps2)]
            for q in range(4):
                mm(br_[:, q, :], BT[0][:, q, :], uT[:, j, :], True, True, *((t_bt,) + free if q == 0 else ()))
                t = mm(bi_[:, q, :], BT[1][:, q, :], uT[:, j, :], True, True, *(free2 if q == 0 else ()), sig=(q == 3))
            return i, i2, br_, bi_, t

        def gelu(j, i, ps, t1):
            y1 = yT[:, j, :]
            t = stt(y1, uT[:, j, :], dsk[:, j:j + 1], ps[:, 0:256], ALU.mult, ALU.add, t1)
            done(i, t)
            tt(gz, y1, y1, ALU.mult)
            ts(gz, gz, 0.044715, 1.0, ALU.mult, ALU.add)
            t = tt(gz, gz, y1, ALU.mult)
            return actf(gz, gz, ACT.Tanh, t, scale=math.sqrt(2 / math.pi))

        def gelu_end(j, t):
            y1 = yT[:, j, :]
            ts(y1, y1, 0.5, None, ALU.mult)
            return stt(y1, gz, 1.0, y1, ALU.add, ALU.mult, t)

        t_ph.append(make_phases(1, None))
        bu = b_times_u(0, turn_b(pad(0, pads[0:2], Bb[0:2], P.last("pe"))))
        before = None
        for j in range(8):
            CC, SS = phases[j % 2]
            M1, M2 = MM[j % 2]
            i, i2, br_, bi_, t = bu
            tt(M1, br_, CC, ALU.mult, t, t_ph[j])
            tt(M2, bi_, SS, ALU.mult)
            tt(Z1, br_, SS, ALU.mult)
            t = tt(Z2, bi_, CC, ALU.mult)
            done(i, t)
            done(i2, t)
            if j < 7:
                got = turn_b(pad(j + 1, pads[0:2], Bb[0:2], P.last("pe")))
            tt(M1, M1, M2, ALU.add)
            tt(M2, Z2, Z1, ALU.subtract)
            if before:
                t_g = gelu(j - 1, *before)
            for q in range(4):
                mg = mag[:, 4 * j + q:4 * j + q + 1].broadcast_to([128, 256])
                scan(Z1[:, q, :], mg, M1[:, q, :], 0.0, ALU.mult, ALU.add)
                scan(Z2[:, q, :], mg, M2[:, q, :], 0.0, ALU.mult, ALU.add)
            if before:
                gelu_end(j - 1, t_g)
            t_pd = pad(j, pads[2:4], (cre, cim))
            if j < 7:
                bu = b_times_u(j + 1, got)
            tt(M1, Z1, CC, ALU.mult)
            tt(M2, Z2, SS, ALU.mult)
            tt(M1, M1, M2, ALU.subtract)
            tt(M2, Z1, SS, ALU.mult)
            t = tt(Z2, Z2, CC, ALU.mult)
            if j < 6:
                t_ph.append(make_phases(j + 2, t))
            t = tt(M2, M2, Z2, ALU.add)
            i, ps, free = pair()
            for q in range(4):
                mm(ps[:, 0:256], pads[2][:, 128 * q:128 * q + 128], M1[:, q, :], q == 0, False,
                   *((t, t_pd) + free if q == 0 else ()))
                t1 = mm(ps[:, 0:256], pads[3][:, 128 * q:128 * q + 128], M2[:, q, :], False, q == 3, sig=(q == 3))
            before = (i, ps, t1)
        t_yT = gelu_end(7, gelu(7, *before))

        gt = MM[0][0]

        def eat_glu(ci, v, t):
            for m in range(4):
                t1 = actf(gt[:, m, :], v[:, m, :], ACT.Sigmoid, t, P.last("dve"), bias=bgl[:, 4 * ci + m:4 * ci + m + 1])
            tt(gt, gt, yT[:, 4 * ci:4 * ci + 4, :], ALU.mult, t1)
            tt(oT[:, 8 + 4 * ci:12 + 4 * ci, :], gt, zb[:, 4 * ci:4 * ci + 4, :], ALU.mult)
            return (t1,)

        proj_b(yT, 8, "w_glu_2", 0, 1024, eat_glu, t_yT)
        t = halve(oT, xT[0], xT[1], P.last("dve"), P.last("pe"))
        proj_a(xT, 16, "w_out_even_2", 0, 2048, eat_out(x, 1.0), t)

        P.barrier()
        top[0] = markh
        hn = tm(2048)
        wt, st = alloc(2048), alloc(64)
        t_h = rms(x, I["norm_odd_g_2"][0], hn, wt, st)
        t_hT_ = to_halves(hn, hT_, 2048, t_h)
        P.barrier()
        top[0] = markh
        qT, kT, zT, oT = fm(16), fm(16), fm(16), fm(16)
        vv = tm(2048)
        fr = at(invm_at, 768).rearrange("p (k t) -> p k t", t=256)
        bf = cols[:, 3:4]
        scs = [alloc(1536), at(xT_at, 1536)]
        pr = alloc(1536).rearrange("p (j t) -> p j t", j=12)
        mxs = [alloc(32).rearrange("p (k b h) -> p k b h", k=4, b=2) for _ in range(2)]
        t_bf = P.loads([(bf[0:16, 0:1], I["b_forget_2"].rearrange("o h -> h o"))])
        sel, t_sel = selector()
        i, ps, t = rows_of("w_in_odd_2", 8192, ((0, 16),), *t_hT_)
        F = [fr[0:16, k, :] for k in range(3)]
        t = ts(F[0], ps[0:16, 0:256], bf[0:16, 0:1], None, ALU.add, None, t, t_bf)
        done(i, t)
        log_sigmoid(F[0], F[1], F[2])
        mset(F[1], 1.0)
        scan(F[0], F[1], F[2], 0.0, ALU.mult, ALU.subtract)
        t_f = P.last("dve")
        proj_b(hT_, 16, "w_in_odd_2", 0, 2048, lambda ci, v, t: (
            copy("act", qT[:, 4 * ci:4 * ci + 4, :], v, t, scale=1.0 / math.sqrt(128.0)),))
        proj_b(hT_, 16, "w_in_odd_2", 2048, 2048, lambda ci, v, t: (copy("act", kT[:, 4 * ci:4 * ci + 4, :], v, t),))
        proj_a(hT_, 16, "w_in_odd_2", 4096, 2048, lambda ci, n, v, t: (copy("act", vv[:, :, 512 * ci:512 * ci + n], v, t),))
        proj_b(hT_, 16, "w_in_odd_2", 6144, 2048, silu_into(zT))
        t_qkv = P.last("act")
        t_za = P.last("dve")

        def odd_scores(u):
            s4 = scs[u % 2].rearrange("p (h x) -> p h x", h=4)
            for g2 in range(2):
                i, ps, free = pair()
                for j in range(2):
                    h = 4 * u + 2 * g2 + j
                    o = ps[:, 512 * j:512 * j + 384]
                    mm(o[:, 0:128], qT[:, h, 0:128], kT[:, h, 0:128], True, False,
                       *(free + (t_qkv, t_f, t_sel) if j == 0 else ()))
                    mm(o[:, 0:128], sel[0:16, h, :], F[0][:, 0:128], False, True)
                    mm(o[:, 128:384], qT[:, h, 128:256], kT[:, h, :], True, False)
                    t = mm(o[:, 128:384], sel[0:16, h, :], F[0], False, True, sig=(j == 1))
                cmb = cmask.unsqueeze(1).broadcast_to([128, 2, 128])
                po = ps.rearrange("p (a x) -> p a x", a=2)
                so = s4[:, 2 * g2:2 * g2 + 2, :]
                tt(so[:, :, 0:128], po[:, :, 0:128], cmb, ALU.add, t, P.last("pe"))
                copy("dve", so[:, :, 128:256], po[:, :, 128:256])
                t1 = tt(so[:, :, 256:384], po[:, :, 256:384], cmb, ALU.add)
                done(i, t1)
            return softmax_exp(u)

        t_e = odd_scores(0)
        for u in range(4):
            t_now = t_e
            if u < 3:
                t_e = odd_scores(u + 1)
            t_pr = softmax_turn(u, t_now)
            for g2 in range(2):
                i, ps, free = pair()
                for j in range(2):
                    m = 2 * g2 + j
                    h = 4 * u + m
                    o = ps[:, 512 * j:512 * j + 256]
                    mm(o, vv[:, 0, 128 * h:128 * h + 128], pr[:, 3 * m:3 * m + 2, :].rearrange("p a t -> p (a t)"),
                       True, False, *(free + (t_pr,) if j == 0 else ()))
                    t = mm(o[:, 128:256], vv[:, 1, 128 * h:128 * h + 128], pr[:, 3 * m + 2, :], False, True,
                           sig=(j == 1))
                hs = slice(4 * u + 2 * g2, 4 * u + 2 * g2 + 2)
                t = tt(oT[:, hs, :], ps.rearrange("p (a x) -> p a x", a=2)[:, :, 0:256], zT[:, hs, :], ALU.mult, t, t_za)
                done(i, t)
        t = halve(oT, xT[0], xT[1], P.last("dve"), P.last("pe"))
        proj_a(xT, 16, "w_out_odd_2", 0, 2048, eat_out(x, 1.0), t)
        P.barrier()
        top[0] = markh
        hn = tm(2048)
        wt, st = alloc(2048), alloc(64)
        t_h = rms(x, I["final_norm_g_2"], hn, wt, st)
        return dump(hn, t_h)


_PLAIN = ["x", "p", "w_in", "mu_shift", "w0", "w_w2", "a0", "w_a2", "w_g2", "k_k", "k_a", "r_k", "lnx_w", "lnx_b",
          "i_bias", "f_bias", "mh_w", "b_gate", "w_br", "w_bm", "w_out", "ln1_w", "ln1_b", "w_rg", "b_rg", "w_re",
          "b_re", "w_gate", "w_up", "w_down", "w_pg", "w_ple", "ln2_w", "ln2_b", "norm_even_g_2", "w_in_even_2",
          "w_glu_2", "w_out_even_2", "norm_odd_g_2", "w_in_odd_2", "b_forget_2", "w_out_odd_2", "final_norm_g_2"]


def kernel(**inputs):
    import numpy as np
    import concourse.bacc as _bacc
    from concourse import mybir as _mybir
    from concourse.bass_utils import run_bass_kernel_spmd as _run

    a = {k: np.ascontiguousarray(inputs[k]) for k in _PLAIN}
    conv = np.concatenate([np.asarray(inputs["conv_w"])[0], np.asarray(inputs["conv_b"])], 0)
    a["conv"] = np.ascontiguousarray(conv.reshape(5, 8, 128).transpose(2, 0, 1))
    rel = np.asarray(inputs["rel_bias_2"])[0]
    idx = np.clip(np.arange(128)[:, None] - np.arange(256)[None, :] + 128, -128, 128) + 128
    a["bias_windows"] = np.ascontiguousarray(rel[:, idx].transpose(1, 0, 2))
    pk = lambda n: np.ascontiguousarray(np.asarray(inputs[n])[0].reshape(32, 128).T)
    a["s5_lr"], a["s5_li"] = pk("s5_lambda_re_2"), pk("s5_lambda_im_2")
    a["s5_ld"] = np.ascontiguousarray(np.asarray(inputs["s5_log_dt_2"])[0].reshape(32, 2).T)
    for k, n in (("s5_bre", "s5_b_re_2"), ("s5_bim", "s5_b_im_2")):
        a[k] = np.ascontiguousarray(np.asarray(inputs[n])[0].reshape(32, 128, 16).transpose(1, 0, 2))
    for k, n in (("s5_cre", "s5_c_re_2"), ("s5_cim", "s5_c_im_2")):
        a[k] = np.ascontiguousarray(
            np.asarray(inputs[n])[0].reshape(32, 2, 16, 64).transpose(1, 3, 0, 2).reshape(128, 32, 16))
    a["s5_dd"] = np.ascontiguousarray(np.asarray(inputs["s5_d_2"])[0].reshape(8, 128).T)
    a["bglu"] = np.ascontiguousarray(np.asarray(inputs["b_glu_2"])[0].reshape(8, 128).T)

    arrays = {"in_" + k: v for k, v in a.items()}
    plan = None
    for _ in range(2):
        nc = _bacc.Bacc("TRN2", target_bir_lowering=False, num_devices=1)
        args = {k: nc.dram_tensor("in_" + k, v.shape, _mybir.dt.from_np(v.dtype), kind="ExternalInput").ap()
                for k, v in a.items()}
        out = nc.dram_tensor("out_0", (1, 256, 2048), _mybir.dt.float32, kind="ExternalOutput").ap()
        plan = build(nc, args, out, plan)
    r = _run(nc, [arrays], core_ids=[0])
    return r.results[0]["out_0"]
```
